# Optimizing a Trainium2 kernel written in Bass

```python
import jax, jax.numpy as jnp
from jax import lax
import numpy as np

D_MODEL = 1024
BATCH = 1
SEQ = 1024
DEPTH = 1

HEAD_DIM = 64
FOX_HEADS = 8
DIL_GROUPS = ((128, 1), (512, 4), (2048, 16))
DIL_HEADS_PER_GROUP = 4
DIL_HEADS = DIL_HEADS_PER_GROUP * len(DIL_GROUPS)
D_FF = 4 * D_MODEL
ROPE_THETA = 500000.0
ROPE_DIM = HEAD_DIM // 4
Q_BLOCK = 128
EPS = 1e-6
NEG_INF = -1e30
FOX_W = FOX_HEADS * HEAD_DIM
DIL_W = DIL_HEADS * HEAD_DIM
DIL_OUT_W = DIL_HEADS_PER_GROUP * HEAD_DIM
IN_SPLIT_SIZES = (FOX_W, FOX_W, FOX_W, FOX_HEADS, DIL_W, DIL_W, DIL_W, D_MODEL, D_MODEL)
D_IN = sum(IN_SPLIT_SIZES)

kernel_name = 'hybrid_fox_dilated_gated_block'

def _rms_norm(x, g):
    xf = x.astype(jnp.float32)
    y = xf * lax.rsqrt(jnp.mean(xf * xf, axis=-1, keepdims=True) + EPS)
    return (y * g.astype(jnp.float32)).astype(x.dtype)

def _partial_rope(x, positions):
    half = ROPE_DIM // 2
    inv_freq = jnp.power(jnp.float32(ROPE_THETA), -jnp.arange(half, dtype=jnp.float32) * 2.0 / ROPE_DIM)
    ang = positions.astype(jnp.float32)[:, None] * inv_freq[None, :]
    cos = jnp.cos(ang)[None, :, None, :]
    sin = jnp.sin(ang)[None, :, None, :]
    xf = x.astype(jnp.float32)
    x1 = xf[..., :half]
    x2 = xf[..., half:ROPE_DIM]
    out = jnp.concatenate([x1 * cos - x2 * sin, x2 * cos + x1 * sin, xf[..., ROPE_DIM:]], axis=-1)
    return out.astype(x.dtype)

def _fox_attention(q, k, v, log_f):
    B, S, H, D = q.shape
    nb = S // Q_BLOCK
    scale = D ** -0.5
    F = jnp.cumsum(log_f, axis=1)
    F_k = jnp.transpose(F, (0, 2, 1))[:, :, None, :]
    k_pos = jnp.arange(S)
    q_blocks = jnp.swapaxes(q.reshape(B, nb, Q_BLOCK, H, D), 0, 1)
    F_blocks = jnp.swapaxes(F.reshape(B, nb, Q_BLOCK, H), 0, 1)

    def one_block(args):
        q_blk, F_blk, i = args
        s = jnp.einsum('bqhd,bkhd->bhqk', q_blk, k, preferred_element_type=jnp.float32) * scale
        s = s + jnp.transpose(F_blk, (0, 2, 1))[..., None] - F_k
        q_pos = i * Q_BLOCK + jnp.arange(Q_BLOCK)
        mask = k_pos[None, :] <= q_pos[:, None]
        s = jnp.where(mask[None, None], s, NEG_INF)
        p = jax.nn.softmax(s, axis=-1)
        return jnp.einsum('bhqk,bkhd->bqhd', p.astype(v.dtype), v)

    out = lax.map(one_block, (q_blocks, F_blocks, jnp.arange(nb)))
    return jnp.swapaxes(out, 0, 1).reshape(B, S, H, D)

def _dilated_group(q, k, v, window, dilation):
    B, S, H, D = q.shape
    L = S // dilation
    W = window // dilation
    blk = W
    Lp = -(-L // blk) * blk
    nb = Lp // blk
    N = B * dilation
    scale = D ** -0.5

    def to_sub(t):
        t = jnp.transpose(t.reshape(B, L, dilation, H, D), (0, 2, 1, 3, 4)).reshape(N, L, H, D)
        t = jnp.pad(t, ((0, 0), (0, Lp - L), (0, 0), (0, 0)))
        return t.reshape(N, nb, blk, H, D)

    def with_prev(t):
        prev = jnp.pad(t[:, :-1], ((0, 0), (1, 0), (0, 0), (0, 0), (0, 0)))
        return jnp.concatenate([prev, t], axis=2)

    qs = to_sub(q)
    k2 = with_prev(to_sub(k))
    v2 = with_prev(to_sub(v))
    s = jnp.einsum('nbqhd,nbkhd->nbhqk', qs, k2, preferred_element_type=jnp.float32) * scale
    a = jnp.arange(blk)
    kk = jnp.arange(2 * blk)
    bidx = jnp.arange(nb)
    diff = blk + a[:, None] - kk[None, :]
    key_idx = bidx[:, None] * blk - blk + kk[None, :]
    mask = ((diff >= 0) & (diff <= W))[None, :, :] & (key_idx >= 0)[:, None, :]
    s = jnp.where(mask[None, :, None], s, NEG_INF)
    m = jnp.max(s, axis=-1, keepdims=True)
    p = jnp.exp(s - m)
    denom = jnp.sum(p, axis=-1, keepdims=True)
    lse = (m + jnp.log(denom))[..., 0]
    out = jnp.einsum('nbhqk,nbkhd->nbqhd', (p / denom).astype(v.dtype), v2)
    out = out.reshape(N, Lp, H, D)[:, :L]
    out = jnp.transpose(out.reshape(B, dilation, L, H, D), (0, 2, 1, 3, 4)).reshape(B, S, H, D)
    lse = jnp.transpose(lse, (0, 1, 3, 2)).reshape(N, Lp, H)[:, :L]
    lse = jnp.transpose(lse.reshape(B, dilation, L, H), (0, 2, 1, 3)).reshape(B, S, H)
    return out, lse

def _dilated_mixture(q, k, v):
    outs, lses = [], []
    for g, (window, dilation) in enumerate(DIL_GROUPS):
        sl = slice(g * DIL_HEADS_PER_GROUP, (g + 1) * DIL_HEADS_PER_GROUP)
        o, lse = _dilated_group(q[:, :, sl], k[:, :, sl], v[:, :, sl], window, dilation)
        outs.append(o)
        lses.append(lse)
    outs = jnp.stack(outs, axis=0)
    alpha = jax.nn.softmax(jnp.stack(lses, axis=0), axis=0)
    return jnp.sum(alpha[..., None].astype(outs.dtype) * outs, axis=0)

def setup_inputs(seed: int = 0) -> dict:
    key = jax.random.key(seed)
    ks = jax.random.split(key, 12)
    f32 = jnp.float32

    def nrm(k, shape, fan_in):
        return jax.random.normal(k, shape, f32) * (fan_in ** -0.5)

    return {
        'x': jax.random.normal(ks[0], (BATCH, SEQ, D_MODEL), f32),
        'norm_attn_g': 1.0 + 0.02 * jax.random.normal(ks[1], (DEPTH, D_MODEL), f32),
        'w_in': nrm(ks[2], (DEPTH, D_MODEL, D_IN), D_MODEL),
        'b_forget': 2.0 + 0.5 * jax.random.normal(ks[3], (DEPTH, FOX_HEADS), f32),
        'w_branch_a': nrm(ks[4], (DEPTH, FOX_W, D_MODEL), FOX_W),
        'w_branch_b': nrm(ks[5], (DEPTH, DIL_OUT_W, D_MODEL), DIL_OUT_W),
        'w_out': nrm(ks[6], (DEPTH, D_MODEL, D_MODEL), D_MODEL),
        'norm_mlp_g': 1.0 + 0.02 * jax.random.normal(ks[7], (DEPTH, D_MODEL), f32),
        'w_up': nrm(ks[8], (DEPTH, D_MODEL, D_FF), D_MODEL),
        'w_down': nrm(ks[9], (DEPTH, D_FF, D_MODEL), D_FF),
        'norm_final_g': 1.0 + 0.02 * jax.random.normal(ks[10], (D_MODEL,), f32),
    }

def reference(x, norm_attn_g, w_in, b_forget, w_branch_a, w_branch_b, w_out,
              norm_mlp_g, w_up, w_down, norm_final_g):
    B, S, _ = x.shape
    positions = jnp.arange(S)
    split_points = [int(v) for v in np.cumsum(IN_SPLIT_SIZES)[:-1]]
    for l in range(DEPTH):
        h = _rms_norm(x, norm_attn_g[l])
        proj = h @ w_in[l]
        qa, ka, va, fa, qb, kb, vb, ga, gb = jnp.split(proj, split_points, axis=-1)
        log_f = jax.nn.log_sigmoid(fa.astype(jnp.float32) + b_forget[l].astype(jnp.float32))
        oa = _fox_attention(qa.reshape(B, S, FOX_HEADS, HEAD_DIM),
                            ka.reshape(B, S, FOX_HEADS, HEAD_DIM),
                            va.reshape(B, S, FOX_HEADS, HEAD_DIM), log_f)
        qb = _partial_rope(qb.reshape(B, S, DIL_HEADS, HEAD_DIM), positions)
        kb = _partial_rope(kb.reshape(B, S, DIL_HEADS, HEAD_DIM), positions)
        ob = _dilated_mixture(qb, kb, vb.reshape(B, S, DIL_HEADS, HEAD_DIM))
        ya = oa.reshape(B, S, FOX_W) @ w_branch_a[l]
        yb = ob.reshape(B, S, DIL_OUT_W) @ w_branch_b[l]
        mixed = jax.nn.sigmoid(ga) * ya + jax.nn.sigmoid(gb) * yb
        x = x + mixed @ w_out[l]
        h = _rms_norm(x, norm_mlp_g[l])
        x = x + jnp.square(jax.nn.relu(h @ w_up[l])) @ w_down[l]
    return _rms_norm(x, norm_final_g)


_drawn_inputs = setup_inputs


def setup_inputs(seed=0):
    import zlib

    import numpy as np

    out = dict(_drawn_inputs(seed))
    spreads = {}
    factors = {'norm_attn_g': 6.822, 'norm_mlp_g': 8.932, 'norm_final_g': 8.483}
    for name, (base, spread) in spreads.items():
        noise = np.random.default_rng([zlib.crc32(name.encode()), seed]).standard_normal(out[name].shape)
        drawn = base * np.exp(spread * noise) if base else spread * noise
        out[name] = __import__('jax').numpy.asarray(drawn.astype(out[name].dtype))
    for name, factor in factors.items():
        out[name] = (out[name] * factor).astype(out[name].dtype)
    return out
```

```python
from contextlib import ExitStack

import concourse.bass as bass
from concourse import mybir

ALU = mybir.AluOpType
ACT = mybir.ActivationFunctionType
BF16 = mybir.dt.bfloat16
F32 = mybir.dt.float32
F32R = mybir.dt.float32r
AX_X = mybir.AxisListType.X

P = 128
D = 1024
S = 1024
KC = D // P
HD = 64
HALF = 512
EPS = 1e-6
NEG = -1e30
FOX_HEADS = 8
FOX_W = FOX_HEADS * HD
DILATIONS = (1, 4, 16)
DIL_W = 4 * HD * len(DILATIONS)
COL_FA = 3 * FOX_W
COL_QB = COL_FA + FOX_HEADS
COL_KB = COL_QB + DIL_W
COL_VB = COL_KB + DIL_W
COL_GA = COL_VB + DIL_W
COL_GB = COL_GA + D
QSCALE = float(HD) ** -0.5
FF_BLOCKS = 8
N_DIL = 2 * len(DILATIONS)
N_FOX = FOX_HEADS // 2
N_GATE = KC
CH0 = 1
CH_OUT = CH0 + 3 * (N_DIL + N_FOX + N_GATE)
PRIME = 1
STEPS = 16


def key_tiles(dil, i):
    if dil is None:
        return [(j, "causal" if j == i else None) for j in range(i + 1)]
    if dil == 16:
        return [(i, "twoblock")]
    if i % (8 // dil) == 0:
        return [(i, "causal")]
    return [(i - 1, "prev"), (i, "causal")]


def units_of(dil, s):
    n = len(key_tiles(dil, s // 2))
    return [(a, min(a + 4, n)) for a in range(0, n, 4)]


def units_before(dil, s):
    return sum(len(units_of(dil, x)) for x in range(s))


def build(nc, x, g_attn, w_in, b_forget, w_branch, w_out, g_mlp, w_up, w_down, g_final, rope, out):
    w_in_v = w_in.rearrange("(k p) n -> p k n", p=P)
    w_br_v = w_branch.rearrange("(k p) n -> p k n", p=P)
    w_out_v = w_out.rearrange("(k p) n -> p k n", p=P)
    w_up_v = w_up.rearrange("(k p) n -> p k n", p=P)
    w_dn_v = w_down.rearrange("(f p) n -> p f n", p=P)
    x_t = x.rearrange("(t p) d -> p t d", p=P)
    out_t = out.rearrange("(t p) d -> p t d", p=P)

    with ExitStack() as ctx:
        def sb(name, shape, dt):
            return ctx.enter_context(nc.sbuf_tensor(name, shape, dt))

        def sem(name):
            return ctx.enter_context(nc.semaphore(name))

        hspl = sb("hspl", [P, 2, KC, S], F32R)
        work = sb("work", [P, 12 * 1024], F32R)
        keep = sb("keep", [P, 8 * 1024], F32)
        raw = sb("raw", [P, 3, 1024], F32)
        wsp = sb("wsp", [P, 3, 2, 1024], F32R)
        tmp = sb("tmp", [P, 4, 1024], F32)
        fbias = sb("fbias", [P, S], BF16)
        fsel = sb("fsel", [P, FOX_HEADS, P], BF16)
        fsel_pair = sb("fsel_pair", [P, 2, P], BF16)
        ident = sb("ident", [P, P], F32)
        ident_b = sb("ident_b", [P, P], BF16)
        masks = sb("masks", [P, 3, P], BF16)
        mean_w = sb("mean_w", [P, P], F32)
        spread_f = sb("spread_f", [P, 2, P], F32)
        spread = sb("spread", [P, 2, P], F32R)
        o_nat = sb("o_nat", [P, 2, P], F32)
        o_part = sb("o_part", [P, 2, HD], F32)
        negmax = sb("negmax", [P, STEPS], F32)
        rowsum = sb("rowsum", [P, STEPS], F32)
        rowinv = sb("rowinv", [P, STEPS], F32)
        st_nm = sb("st_nm", [P, 3, 8, 2, 2], F32)
        st_rs = sb("st_rs", [P, 3, 8, 2, 2], F32)
        xstat = sb("xstat", [P, KC], F32)
        xrstd = sb("xrstd", [P, KC], F32)
        ga_g = sb("ga_g", [P, KC], F32)
        gm_g = sb("gm_g", [P, KC], F32)
        eps_c = sb("eps_c", [P, 1], F32)
        bfor = sb("bfor", [P, 1], F32)
        PS = [ctx.enter_context(nc.psum_tensor(f"ps{i}", [P, 1024], F32)) for i in range(4)]
        MASK = {"causal": masks[:, 0, :], "prev": masks[:, 1, :], "twoblock": masks[:, 2, :]}

        k_st = [work[:, h * 1024:(h + 1) * 1024] for h in range(2)]
        q_hi = [work[:, (2 + h) * 1024:(3 + h) * 1024] for h in range(2)]
        q_lo = [work[:, (4 + h) * 1024:(5 + h) * 1024] for h in range(2)]
        v_nat = work[:, 6 * 1024:8 * 1024].rearrange("p (t h s d) -> p t h s d", t=8, h=2, s=2)
        pt = work[:, 8 * 1024:12 * 1024].rearrange("p (b s c) -> p b s c", b=2, s=2)
        alpha_st = work[:, 0:3072].rearrange("p (g c) -> p g c", g=3)
        br_in = work[:, :].rearrange("p (s k c) -> p s k c", s=2, k=6)
        hid = work[:, 0:8192].rearrange("p (s f c) -> p s f c", s=2, f=4)

        og = keep[:, 0:6144].rearrange("p (g c) -> p g c", g=3)
        ob = keep[:, 6144:8192]
        kp = keep[:, :].rearrange("p (k c) -> p k c", k=KC)

        def raw_at(n):
            return tmp[:, 2, :] if n % 4 == 3 else raw[:, n % 4, :]

        def wsp_at(n, part):
            return work[:, 8192 + part * 1024:9216 + part * 1024] if n % 4 == 3 else wsp[:, n % 4, part, :]

        x_in = [sem(f"x_in{i}") for i in range(4)]
        small_in = sem("small_in")
        rope_in = sem("rope_in")
        xcol_in = sem("xcol_in")
        gfin_in = sem("gfin_in")
        w_in_s = [sem(f"w_loaded{i}") for i in range(4)]
        w_hi = sem("w_hi")
        w_lo = sem("w_lo")
        w_used = sem("w_used")
        consts = sem("consts")
        fsel_ok = sem("fsel_ok")
        spread_ok = sem("spread_ok")
        x_sq = sem("x_sq")
        x_st = sem("x_st")
        x_root = sem("x_root")
        x_rs = sem("x_rs")
        x_scaled = sem("x_scaled")
        xt_done = sem("xt_done")
        xhi = sem("xhi")
        xlo = sem("xlo")
        dchain = sem("dchain")
        achain = sem("achain")
        fz_ok = sem("fz_ok")
        fln_ok = sem("fln_ok")
        fbias_ok = sem("fbias_ok")
        raw_out = sem("raw_out")
        roped = sem("roped")
        st_hi = sem("st_hi")
        st_lo = sem("st_lo")
        vt_done = sem("vt_done")
        v_hi = sem("v_hi")
        v_lo = sem("v_lo")
        sel_ok = sem("sel_ok")
        qk_done = sem("qk_done")
        max_done = sem("max_done")
        exp_done = sem("exp_done")
        inv_done = sem("inv_done")
        tr_done = sem("tr_done")
        pt_hi = sem("pt_hi")
        pt_lo = sem("pt_lo")
        pv_done = sem("pv_done")
        op_done = sem("op_done")
        on_done = sem("on_done")
        ot_done = sem("ot_done")
        ote_done = sem("ote_done")
        stat_ok = sem("stat_ok")
        alpha0 = sem("alpha0")
        ln_ok = sem("ln_ok")
        lse_ok = sem("lse_ok")
        lt_done = sem("lt_done")
        lt_out = sem("lt_out")
        lsub_ok = sem("lsub_ok")
        lexp_ok = sem("lexp_ok")
        alpha_f = sem("alpha_f")
        alpha_hi = sem("alpha_hi")
        alpha_ok = sem("alpha_ok")
        spr_done = sem("spr_done")
        spr_out = sem("spr_out")
        comb_ok = sem("comb_ok")
        br_hi = sem("br_hi")
        br_lo = sem("br_lo")
        sig_ok = sem("sig_ok")
        gmul = sem("gmul")
        mixed_ok = sem("mixed_ok")
        m_hi = sem("m_hi")
        m_lo = sem("m_lo")
        xct_done = sem("xct_done")
        xres = sem("xres")
        resid = sem("resid")
        sq_ok = sem("sq_ok")
        acc_ok = sem("acc_ok")
        mean_done = sem("mean_done")
        mean_out = sem("mean_out")
        rstd_ok = sem("rstd_ok")
        h_hi = sem("h_hi")
        h_lo = sem("h_lo")
        u_r = sem("u_r")
        u_sq = sem("u_sq")
        u_hi = sem("u_hi")
        u_lo = sem("u_lo")
        dn_even = sem("dn_even")
        dn_add = sem("dn_add")
        fsq = sem("fsq")
        facc = sem("facc")
        fmean = sem("fmean")
        fmean_out = sem("fmean_out")
        froot = sem("froot")
        frstd = sem("frstd")
        ft_done = sem("ft_done")
        y_ok = sem("y_ok")
        y_out = [sem(f"y_out{i}") for i in range(2)]

        block = ctx.enter_context(nc.Block())

        @block.sync
        def _(sp):
            def load_chunk(slot, src, dst=None):
                dst = raw[:, slot, :] if dst is None else dst
                n = src.shape[1] * src.shape[2]
                sp.dma_start(dst[:, 0:n].rearrange("p (k c) -> p k c", k=src.shape[1]), src).then_inc(w_in_s[slot], 16)

            for i in range(4):
                sp.dma_start(tmp[:, i, :], x_t[:, i, :]).then_inc(x_in[i], 16)
            sp.dma_start(ga_g[:], g_attn).then_inc(small_in, 16)
            sp.dma_start(gm_g[:], g_mlp).then_inc(small_in, 16)
            sp.dma_start(bfor[0:FOX_HEADS, :], b_forget).then_inc(small_in, 16)
            load_chunk(2, w_in_v[:, :, COL_FA:COL_FA + P])
            load_chunk(0, w_in_v[:, :, COL_QB:COL_QB + P])
            load_chunk(1, w_in_v[:, :, COL_KB:COL_KB + P])
            sp.wait_ge(xt_done, 8)
            for i in range(4):
                sp.dma_start(tmp[:, i, :], x_t[:, 4 + i, :]).then_inc(x_in[i], 16)
            sp.wait_ge(w_lo, 1)
            load_chunk(2, w_in_v[:, :, COL_VB:COL_VB + P])
            sp.wait_ge(fbias_ok, 1)
            sp.dma_start(tmp[:, 2:4, :], rope).then_inc(rope_in, 16)
            for t in range(1, N_DIL):
                for j, col in enumerate((COL_QB, COL_KB, COL_VB)):
                    sp.wait_ge(w_lo, CH0 + 3 * (t - 1) + j + 1)
                    load_chunk(j, w_in_v[:, :, col + t * P:col + (t + 1) * P])
            for t in range(N_DIL, N_DIL + N_FOX + N_GATE):
                m = (t - N_DIL if t < N_DIL + N_FOX else t - N_DIL - N_FOX) * P
                if t < N_DIL + N_FOX:
                    srcs = [w_in_v[:, :, m + j * FOX_W:m + j * FOX_W + P] for j in range(3)]
                else:
                    srcs = [w_in_v[:, :, COL_GA + m:COL_GA + m + P], w_in_v[:, :, COL_GB + m:COL_GB + m + P],
                            w_br_v[:, :, m:m + P]]
                for j in range(3):
                    sp.wait_ge(w_lo, CH0 + 3 * (t - 1) + j + 1)
                    load_chunk(j, srcs[j])

            def xcol(m):
                sp.dma_start(tmp[:, 0, :].rearrange("p (t c) -> p t c", t=8),
                             x_t[:, :, bass.ds(m * P, P) if not isinstance(m, int) else slice(m * P, m * P + P)]
                             ).then_inc(xcol_in, 16)

            for n in range(3):
                sp.wait_ge(w_lo, CH_OUT - 3 + n + 1)
                load_chunk(n, w_out_v[:, :, n * P:(n + 1) * P])
            sp.wait_ge(mixed_ok, N_GATE + PRIME)
            xcol(0)
            for n in range(KC):
                if n < KC - 1:
                    sp.wait_ge(xct_done, n + 1)
                    xcol(n + 1)
                if n + 3 < KC:
                    sp.wait_ge(w_lo, CH_OUT + n)
                    load_chunk((n + 3) % 4, w_out_v[:, :, (n + 3) * P:(n + 4) * P], raw_at(n + 3))
            with sp.Fori(0, FF_BLOCKS) as b:
                for c in range(8):
                    sp.wait_ge(w_lo, b * 8 + (CH_OUT + KC + c - 4 + 1))
                    if c < 4:
                        src = w_up_v[:, :, bass.ds(b * 512 + c * P, P)]
                    else:
                        src = w_dn_v[:, bass.ds(b * 4, 4), (c - 4) * 256:(c - 3) * 256]
                    load_chunk(c % 4, src, raw_at(c))
            sp.wait_ge(w_lo, CH_OUT + KC + 8 * FF_BLOCKS)
            sp.dma_start(tmp[:, 2, :], g_final).then_inc(gfin_in, 16)
            for i in range(8):
                sp.wait_ge(y_ok, i + 1)
                sp.dma_start(out_t[:, i, :], tmp[:, i % 2, :]).then_inc(y_out[i % 2], 16)
            for i in range(2):
                sp.wait_ge(y_out[i], 16 * 4)

        @block.gpsimd
        def _(pool):
            n = [0]

            def step(ins):
                n[0] += 1
                ins.then_inc(consts, 1)

            def settle():
                pool.wait_ge(consts, n[0])

            step(pool.memset(ident[:], 0.0))
            step(pool.memset(ident_b[:], 0.0))
            step(pool.memset(masks[:], 0.0))
            step(pool.memset(mean_w[:], 1.0 / D))
            step(pool.memset(eps_c[:], EPS))
            step(pool.memset(fbias[:], 0.0))
            step(pool.memset(fsel[:], 0.0))
            step(pool.memset(spread_f[:], 0.0))
            settle()
            for m in (ident, ident_b):
                step(pool.affine_select(out=m[:], in_=m[:], compare_op=ALU.not_equal, fill=1.0, base=0,
                                        pattern=[[-1, P]], channel_multiplier=1))
            step(pool.affine_select(out=masks[:, 0, :], in_=masks[:, 0, :], compare_op=ALU.is_ge, fill=NEG,
                                    base=0, pattern=[[-1, P]], channel_multiplier=1))
            step(pool.affine_select(out=masks[:, 1, :], in_=masks[:, 1, :], compare_op=ALU.is_ge, fill=NEG,
                                    base=0, pattern=[[1, P]], channel_multiplier=-1))
            step(pool.affine_select(out=masks[:, 2, :], in_=masks[:, 2, :], compare_op=ALU.is_ge, fill=NEG,
                                    base=0, pattern=[[-1, P]], channel_multiplier=1))
            settle()
            step(pool.affine_select(out=masks[:, 2, 0:64], in_=masks[:, 2, 0:64], compare_op=ALU.is_ge, fill=NEG,
                                    base=63, pattern=[[0, 64]], channel_multiplier=-1))
            for r in range(3):
                settle()
                step(pool.affine_select(out=fsel[:], in_=fsel[:], compare_op=ALU.not_equal, fill=1.0, base=-32 * r,
                                        pattern=[[-1, FOX_HEADS], [0, P]], channel_multiplier=1))
            sv = spread_f[:].rearrange("p a (h d) -> p a h d", h=2)
            for r in range(2):
                settle()
                step(pool.affine_select(out=sv, in_=sv, compare_op=ALU.not_equal, fill=1.0, base=-32 * r,
                                        pattern=[[-2, 2], [-1, 2], [0, HD]], channel_multiplier=1))
            pool.wait_ge(pv_done, STEPS * N_DIL + PRIME)
            pool.memset(alpha_st.bitcast(F32), 0.0).then_inc(alpha0, 1)

        N_CONST = 8 + 5 + 1 + 3 + 2

        @block.tensor
        def _(pe):
            for primed in (qk_done, tr_done, pv_done):
                pe.sem_inc(primed, 1)
            def split_products(ps, w, mv, ks, last_inc=None):
                ins = None
                for half in range(2):
                    cols = slice(half * HALF, (half + 1) * HALF)
                    for k in range(ks):
                        for n, (wp, mp) in enumerate(((0, 0), (0, 1), (1, 0))):
                            ins = pe.matmul(ps[:, cols], w(wp, k), mv(mp, k)[:, cols],
                                            start=(k == 0 and n == 0), stop=(k == ks - 1 and n == 2))
                return ins

            def w_tri(j):
                return lambda part, k: wsp[:, j, part, k * P:(k + 1) * P]

            def h_at(part, k):
                return hspl[:, part, k, :]

            pe.wait_ge(consts, N_CONST)
            for half in range(2):
                for c in range(KC):
                    n = half * KC + c
                    if c == 0:
                        pe.wait_ge(x_scaled, 4 * half + 4)
                    if n >= 4:
                        pe.wait_ge(xlo, n - 3)
                    bank = PS[(n % 4) // 2][:, (n % 2) * HALF:(n % 2 + 1) * HALF]
                    for t in range(4):
                        ins = pe.transpose(bank[:, t * P:(t + 1) * P], tmp[:, t, c * P:(c + 1) * P], ident[:])
                    ins.then_inc(xt_done, 1)
            pe.wait_ge(xlo, 16)
            pe.wait_ge(w_lo, 1)
            split_products(PS[0], w_tri(2), h_at, KC).then_inc(w_used, 1)

            def attention(dil, t, ub):
                for j in range(3):
                    if j < 2:
                        pe.wait_ge(exp_done, t * STEPS + PRIME)
                    else:
                        pe.wait_ge(raw_out, t * 3 + 1)
                    pe.wait_ge(w_lo, t * 3 + (CH0 + j + 1))
                    split_products(PS[j % 2], w_tri(j), h_at, KC).then_inc(w_used, 1)
                pe.wait_ge(raw_out, t * 3 + 3)
                pe.wait_ge(pt_lo, ub + PRIME)
                for i in range(8):
                    ins = pe.transpose(PS[2][:, i * P:(i + 1) * P], tmp[:, 0, i * P:(i + 1) * P], ident[:])
                    if i % 4 == 3:
                        ins.then_inc(vt_done, 1)

                def scores(s):
                    i, h = divmod(s, 2)
                    tiles = key_tiles(dil, i)
                    if s == 0:
                        pe.wait_ge(st_lo, t * 6 + 6)
                        if dil is None:
                            pe.wait_ge(sel_ok, t - (N_DIL - 1))
                    if s >= 2:
                        pe.wait_ge(exp_done, t * STEPS + (s - 1) + PRIME)
                    ps = PS[h]
                    base = tiles[0][0]
                    end = tiles[-1][0] + 1 - base
                    for c0 in range(0, end, 4):
                        n = min(4, end - c0)
                        o = ps[:, c0 * P:(c0 + n) * P]
                        kc = slice((base + c0) * P, (base + c0 + n) * P)
                        ops = [(q_hi[h][:, i * P:(i + 1) * P], k_st[h][:, kc], o),
                               (q_lo[h][:, i * P:(i + 1) * P], k_st[h][:, kc], o)]
                        if dil is None:
                            ops.append((fsel_pair[:, h, :], fbias[:, kc], o))
                        for j, mask in tiles:
                            if mask and c0 <= j - base < c0 + n:
                                a = (j - base) * P
                                ops.append((ident_b[:], MASK[mask], ps[:, a:a + P]))
                        for m, (lt, rh, oo) in enumerate(ops):
                            ins = pe.matmul(oo, lt, rh, start=(m == 0), stop=(m == len(ops) - 1),
                                            skip_group_check=True)
                    ins.then_inc(qk_done, 1)

                def transposes(s):
                    pe.wait_ge(exp_done, t * STEPS + s + 1 + PRIME)
                    for n, (a, b) in enumerate(units_of(dil, s)):
                        u = units_before(dil, s) + n
                        if u < 2:
                            pe.wait_ge(v_lo, t * 2 + u + 1)
                        else:
                            pe.wait_ge(pt_lo, ub + (u - 1) + PRIME)
                        for k in range(a, b):
                            ins = pe.transpose(PS[2][:, (u % 2) * HALF + (k - a) * P:(u % 2) * HALF + (k - a + 1) * P],
                                               tmp[:, s % 2, k * P:(k + 1) * P], ident[:])
                        ins.then_inc(tr_done, 1)

                def values(s):
                    i, h = divmod(s, 2)
                    tiles = key_tiles(dil, i)
                    pe.wait_ge(pt_lo, ub + units_before(dil, s + 1) + PRIME)
                    if s == 0:
                        pe.wait_ge(v_lo, t * 2 + 2)
                        pe.wait_ge(on_done, t * STEPS + PRIME)
                    if s >= 2:
                        pe.wait_ge(on_done, t * STEPS + (s - 1) + PRIME)
                    if h == 0:
                        pe.wait_ge(ote_done, t * 8 + i + PRIME)
                    o = PS[3][:, h * HALF:h * HALF + P]
                    for part in range(2):
                        for n, (j, _) in enumerate(tiles):
                            ins = pe.matmul(o, pt[:, s % 2, part, n * P:(n + 1) * P],
                                            v_nat[:, j, h, :, :].rearrange("p s d -> p (s d)"),
                                            start=(part == 0 and n == 0), stop=(part == 1 and n == len(tiles) - 1))
                    ins.then_inc(pv_done, 1)

                def out_transpose(i):
                    pe.wait_ge(on_done, t * STEPS + (2 * i + 2) + PRIME)
                    pe.transpose(PS[3][:, 256:256 + P], o_nat[:, i % 2, :], ident[:]).then_inc(ot_done, 1)

                for s in range(STEPS + 3):
                    if s < STEPS:
                        scores(s)
                    if s >= 4 and s % 2 == 0:
                        out_transpose((s - 4) // 2)
                    if 1 <= s <= STEPS:
                        transposes(s - 1)
                    if 2 <= s < STEPS + 2:
                        values(s - 2)

            pe.wait_ge(fz_ok, 1)
            for g, dil in enumerate(DILATIONS):
                with pe.Fori(0, 2) as pair:
                    attention(dil, pair + 2 * g, (pair + 2 * g) * 16)

            pe.wait_ge(lse_ok, 1)
            pe.wait_ge(pt_lo, 16 * N_DIL + PRIME)
            pe.wait_ge(ote_done, 8 * N_DIL + PRIME)
            lse_v = st_rs[:].rearrange("p g i a h -> p g i (a h)")
            for g in range(3):
                if g == 2:
                    pe.wait_ge(lt_out, 1)
                for i in range(8):
                    ins = pe.transpose(PS[2 + g % 2][0:4, i * P:(i + 1) * P], lse_v[:, g, i, :], ident[:])
                ins.then_inc(lt_done, 1)
            pe.wait_ge(alpha_ok, 1)
            pe.wait_ge(spread_ok, 1)
            for n in range(6):
                pair, g = divmod(n, 3)
                if n >= 2:
                    pe.wait_ge(spr_out, n - 1)
                for half in range(2):
                    cols = slice(half * HALF, (half + 1) * HALF)
                    ins = pe.matmul(PS[n % 2][:, cols], spread[:, pair, :], alpha_st[:, g, cols], start=True, stop=True)
                ins.then_inc(spr_done, 1)
            pe.wait_ge(spr_out, 6)

            with pe.Fori(0, N_FOX) as it:
                attention(None, it + N_DIL, it * 24 + 16 * N_DIL)

            T0 = N_DIL + N_FOX
            pe.wait_ge(exp_done, STEPS * T0 + PRIME)
            pe.wait_ge(pt_lo, 16 * N_DIL + 24 * N_FOX + PRIME)
            pe.wait_ge(ote_done, 8 * T0 + PRIME)
            with pe.Fori(0, N_GATE) as it:
                for j in range(2):
                    pe.wait_ge(sig_ok, it * 2 + j + PRIME)
                    pe.wait_ge(w_lo, it * 3 + (CH0 + 3 * T0 + j + 1))
                    split_products(PS[j], w_tri(j), h_at, KC).then_inc(w_used, 1)
                pe.wait_ge(br_lo, 6)
                pe.wait_ge(gmul, it * 2 + PRIME)
                pe.wait_ge(w_lo, it * 3 + (CH0 + 3 * T0 + 3))
                split_products(PS[2], w_tri(2), lambda part, k: br_in[:, part, k, :], 4)
                split_products(PS[3], lambda part, k: wsp[:, 2, part, (4 + k) * P:(5 + k) * P],
                               lambda part, k: br_in[:, part, 4 + k, :], 2).then_inc(w_used, 1)

            pe.wait_ge(gmul, 2 * N_GATE + PRIME)
            pe.wait_ge(sig_ok, 2 * N_GATE + PRIME)
            for n in range(KC):
                pe.wait_ge(xcol_in, 16 * (n + 1))
                if n >= 2:
                    pe.wait_ge(xres, n - 1)
                for t in range(8):
                    ins = pe.transpose(PS[2 + n % 2][:, t * P:(t + 1) * P], tmp[:, 0, t * P:(t + 1) * P], ident[:])
                ins.then_inc(xct_done, 1)
                pe.wait_ge(w_lo, CH_OUT + n + 1)
                if n >= 2:
                    pe.wait_ge(resid, n - 1)
                if n == 0:
                    pe.wait_ge(m_lo, KC)
                split_products(PS[n % 2], lambda part, k: wsp_at(n, part)[:, k * P:(k + 1) * P], h_at,
                               KC).then_inc(w_used, 1)

            def mean_square(done):
                for half in range(2):
                    cols = slice(half * HALF, (half + 1) * HALF)
                    ins = pe.matmul(PS[0][:, cols], mean_w[:], tmp[:, 3, cols], start=True, stop=True)
                ins.then_inc(done, 1)

            pe.wait_ge(resid, KC)
            pe.wait_ge(acc_ok, KC + 1)
            mean_square(mean_done)

            with pe.Fori(0, FF_BLOCKS) as b:
                for j in range(4):
                    if j == 0:
                        pe.wait_ge(h_lo, KC)
                        pe.wait_ge(mean_out, 1)
                    if j < 2:
                        pe.wait_ge(u_r, b * 4 + PRIME)
                    else:
                        pe.wait_ge(u_r, b * 4 + (j - 1) + PRIME)
                    pe.wait_ge(w_lo, b * 8 + (CH_OUT + KC + j + 1))
                    split_products(PS[j % 2], lambda part, k: wsp_at(j, part)[:, k * P:(k + 1) * P], h_at,
                                   KC).then_inc(w_used, 1)
                for m in range(8):
                    if m % 2 == 0:
                        pe.wait_ge(w_lo, b * 8 + (CH_OUT + KC + 4 + m // 2 + 1))
                    if m < 2:
                        pe.wait_ge(dn_add, b * 8 + PRIME)
                    else:
                        pe.wait_ge(dn_add, b * 8 + (m - 1) + PRIME)
                    for half in range(2):
                        cols = slice(half * HALF, (half + 1) * HALF)
                        for f in range(4):
                            if m == 0:
                                pe.wait_ge(u_lo, b * 4 + (f + 1) + PRIME)
                            for n, (wp, mp) in enumerate(((0, 0), (0, 1), (1, 0))):
                                a = f * 256 + (m % 2) * P
                                ins = pe.matmul(PS[2 + m % 2][:, cols], wsp_at(m // 2, wp)[:, a:a + P],
                                                hid[:, mp, f, cols],
                                                start=(f == 0 and n == 0), stop=(f == 3 and n == 2))
                    ins.then_inc(w_used if m % 2 else dn_even, 1)

            pe.wait_ge(facc, KC)
            for i in range(8):
                ins = pe.matmul(PS[0][:, i:i + 1], tmp[:, 3, i * P:(i + 1) * P], mean_w[:, 0:1], start=True, stop=True)
            ins.then_inc(fmean, 1)
            for i in range(8):
                if i >= 3:
                    pe.wait_ge(y_ok, i - 2)
                for c in range(KC):
                    ins = pe.transpose(PS[1 + i % 3][:, c * P:(c + 1) * P], kp[:, c, i * P:(i + 1) * P], ident[:])
                ins.then_inc(ft_done, 1)

        @block.scalar
        def _(act):
            for primed in (exp_done, ote_done, sig_ok, u_sq):
                act.sem_inc(primed, 1)
            chain = [0]

            def link(ins):
                chain[0] += 1
                ins.then_inc(achain, 1)
                act.wait_ge(achain, chain[0])

            def split_hi(slot, loads, chunk, used):
                act.wait_ge(w_in_s[slot], loads)
                act.wait_ge(w_used, used)
                act.copy(wsp[:, slot, 0, :], raw[:, slot, :]).then_inc(w_hi, 1)

            for half in range(2):
                for i in range(4):
                    act.wait_ge(x_in[i], 16 * (half + 1))
                    act.wait_ge(x_sq, 4 * half + i)
                    act.activation(PS[3][:], tmp[:, i, :], ACT.Square,
                                   accum_out=xstat[:, 4 * half + i:4 * half + i + 1]).then_inc(x_sq, 1)
                act.wait_ge(x_st, half + 1)
                act.activation(xstat[:, 4 * half:4 * half + 4], xstat[:, 4 * half:4 * half + 4],
                               ACT.Sqrt).then_inc(x_root, 1)
                if half == 0:
                    act.wait_ge(small_in, 48)
                    split_hi(2, 16, 0, 0)
                else:
                    split_hi(0, 16, 1, 0)
                    split_hi(1, 16, 2, 0)
                for c in range(KC):
                    n = half * KC + c
                    act.wait_ge(xt_done, n + 1)
                    bank = PS[(n % 4) // 2][:, (n % 2) * HALF:(n % 2 + 1) * HALF]
                    act.activation(hspl[:, 0, c, half * HALF:(half + 1) * HALF], bank, ACT.Copy,
                                   scale=ga_g[:, c:c + 1]).then_inc(xhi, 1)
            act.wait_ge(consts, N_CONST)
            act.copy(spread[:], spread_f[:]).then_inc(spread_ok, 1)
            act.wait_ge(fz_ok, 1)
            fz, fe = tmp[0:FOX_HEADS, 0, :], tmp[0:FOX_HEADS, 1, :]
            link(act.activation(fe, fz, ACT.Abs))
            link(act.activation(fe, fe, ACT.Exp, scale=-1.0))
            act.activation(fe, fe, ACT.Ln, bias=1.0).then_inc(fln_ok, 1)
            split_hi(2, 32, 3, 1)

            def attention(dil, t, ub):
                perm = (lambda ap: ap) if dil in (None, 1) else (lambda ap: ap.rearrange("p (l r) -> p r l", r=dil))
                view = (lambda ap: ap) if dil in (None, 1) else (lambda ap: ap.rearrange("p (r l) -> p r l", r=dil))
                for j in range(2):
                    if dil is None:
                        act.wait_ge(w_used, t * 3 + (CH0 + j + 1))
                        act.wait_ge(tr_done, ub + PRIME)
                        act.copy(tmp[:, j, :], PS[j][:]).then_inc(raw_out, 1)
                    act.wait_ge(raw_out, t * 3 + j + 1)
                    if j == 0:
                        act.wait_ge(qk_done, t * STEPS + PRIME)
                        dsts = [(q_hi[0][0:64], 0), (q_hi[0][64:P], 0), (q_hi[1][64:P], 64), (q_hi[1][0:64], 64)]
                    else:
                        dsts = [(k_st[0][0:64], 0), (k_st[1][64:P], 64)]
                    for dst, row in dsts:
                        act.activation(view(dst), perm(tmp[row:row + 64, j, :]), ACT.Copy,
                                       scale=QSCALE if j == 0 else 1.0).then_inc(st_hi, 1)
                act.wait_ge(w_used, t * 3 + (CH0 + 3))
                act.wait_ge(st_lo, t * 6 + 4)
                if dil is not None:
                    act.wait_ge(raw_out, t * 3 + 2)
                act.copy(view(tmp[:, 0, :]), perm(PS[0][:])).then_inc(raw_out, 1)
                for bank in range(2):
                    act.wait_ge(vt_done, t * 2 + bank + 1)
                    act.wait_ge(pv_done, t * STEPS + PRIME)
                    act.copy(v_nat[:, 4 * bank:4 * bank + 4, :, 0, :],
                             PS[2][:, bank * HALF:(bank + 1) * HALF].rearrange("p (t h d) -> p t h d", t=4, h=2)
                             ).then_inc(v_hi, 1)
                if dil is None:
                    act.copy(fsel_pair[:], fsel[:, bass.ds((t - N_DIL) * 2, 2), :]).then_inc(sel_ok, 1)

                def exps(s):
                    n = len(key_tiles(dil, s // 2))
                    act.wait_ge(max_done, t * STEPS + s + 1)
                    if s == 0:
                        act.wait_ge(vt_done, t * 2 + 2)
                        act.wait_ge(stat_ok, (t if dil is not None else N_DIL) + PRIME)
                    elif s == 1:
                        act.wait_ge(st_lo, t * 6 + 6)
                    else:
                        act.wait_ge(tr_done, ub + units_before(dil, s - 1) + PRIME)
                    act.activation(tmp[:, s % 2, 0:n * P], PS[s % 2][:, 0:n * P], ACT.Exp,
                                   bias=negmax[:, s:s + 1], accum_out=rowsum[:, s:s + 1]).then_inc(exp_done, 1)

                def probs_hi(s):
                    for n, (a, b) in enumerate(units_of(dil, s)):
                        u = units_before(dil, s) + n
                        act.wait_ge(tr_done, ub + (u + 1) + PRIME)
                        if s >= 2:
                            act.wait_ge(pv_done, t * STEPS + (s - 1) + PRIME)
                        act.copy(pt[:, s % 2, 0, a * P:b * P],
                                 PS[2][:, (u % 2) * HALF:(u % 2) * HALF + (b - a) * P]).then_inc(pt_hi, 1)

                def out_part(s):
                    h = s % 2
                    act.wait_ge(pv_done, t * STEPS + s + 1 + PRIME)
                    act.wait_ge(inv_done, t * STEPS + s + 1)
                    if s >= 2:
                        act.wait_ge(on_done, t * STEPS + (s - 1) + PRIME)
                    act.activation(o_part[:, h, :], PS[3][:, h * HALF + HD:h * HALF + P], ACT.Copy,
                                   scale=rowinv[:, s:s + 1]).then_inc(op_done, 1)

                def out_store(i):
                    act.wait_ge(ot_done, t * 8 + (i + 1))
                    src = PS[3][:, 256:256 + P]
                    if dil is None:
                        dst = keep[:, bass.ds((t - N_DIL) * 1024 + i * P, P)]
                    else:
                        g = DILATIONS.index(dil)
                        dst = og[:, g, bass.ds((t - 2 * g) * 1024, 1024)]
                        if dil == 1:
                            dst = dst[:, i * P:(i + 1) * P]
                        elif dil == 4:
                            dst = dst.rearrange("p (l r) -> p r l", r=4)[:, i // 2, (i % 2) * P:(i % 2 + 1) * P]
                        else:
                            dst = dst.rearrange("p (l r) -> p r l", r=16)[:, 2 * i:2 * i + 2, :]
                            src = src.rearrange("p (r l) -> p r l", r=2)
                    act.copy(dst, src).then_inc(ote_done, 1)

                for s in range(STEPS + 3):
                    if s < STEPS:
                        exps(s)
                    if s >= 4 and s % 2 == 0:
                        out_store((s - 4) // 2)
                    if 1 <= s <= STEPS:
                        probs_hi(s - 1)
                    if 2 <= s < STEPS + 2:
                        out_part(s - 2)
                    if s in (3, 8, 12):
                        j = (3, 8, 12).index(s)
                        split_hi(j, t * 16 + (32 if j < 2 else 48), None, t * 3 + (CH0 + j + 1))

            for g, dil in enumerate(DILATIONS):
                with act.Fori(0, 2) as pair:
                    attention(dil, pair + 2 * g, (pair + 2 * g) * 16)

            act.wait_ge(stat_ok, N_DIL + PRIME)
            act.activation(st_rs[:], st_rs[:], ACT.Ln).then_inc(ln_ok, 1)
            act.wait_ge(lsub_ok, 1)
            act.activation(tmp[0:4, 0:3, :], tmp[0:4, 0:3, :], ACT.Exp).then_inc(lexp_ok, 1)
            act.wait_ge(alpha_f, 1)
            act.wait_ge(alpha0, 1)
            act.copy(alpha_st[0:4], tmp[0:4, 0:3, :]).then_inc(alpha_hi, 1)
            act.wait_ge(comb_ok, 1)
            with act.Fori(0, N_FOX) as it:
                attention(None, it + N_DIL, it * 24 + 16 * N_DIL)

            T0 = N_DIL + N_FOX
            act.wait_ge(pv_done, STEPS * T0 + PRIME)
            act.wait_ge(ote_done, 8 * T0 + PRIME)
            for k in range(6):
                src = keep[:, k * 1024:(k + 1) * 1024] if k < 4 else ob[:, (k - 4) * 1024:(k - 3) * 1024]
                act.copy(br_in[:, 0, k, :], src).then_inc(br_hi, 1)
            with act.Fori(0, N_GATE) as it:
                for j in range(2):
                    act.wait_ge(w_used, it * 3 + (CH0 + 3 * T0 + j + 1))
                    act.wait_ge(mixed_ok, it + PRIME)
                    act.activation(tmp[:, j, :], PS[j][:], ACT.Sigmoid).then_inc(sig_ok, 1)
                    split_hi(j, it * 16 + 16 * (T0 + 2), None, it * 3 + (CH0 + 3 * T0 + j + 1))
                split_hi(2, it * 16 + 16 * (T0 + 3), None, it * 3 + (CH0 + 3 * T0 + 3))

            act.wait_ge(w_used, CH_OUT)
            for c in range(KC):
                act.wait_ge(mixed_ok, N_GATE + PRIME)
                act.copy(hspl[:, 0, c, :], kp[:, c, :]).then_inc(m_hi, 1)

            def loads(n):
                return 16 * ((N_DIL + N_FOX + N_GATE, N_DIL + N_FOX + N_GATE, N_DIL + N_FOX + N_GATE + 1, 0)[n % 4]
                             + n // 4 + 1)

            def split_hi2(n, b=None):
                if b is None:
                    act.wait_ge(w_in_s[n % 4], loads(n))
                    act.wait_ge(w_used, CH_OUT + n - 3)
                else:
                    act.wait_ge(w_in_s[n % 4], b * 32 + loads(n))
                    act.wait_ge(w_used, b * 8 + (CH_OUT + n - 3))
                act.copy(wsp_at(n, 0), raw_at(n)).then_inc(w_hi, 1)

            for n in range(KC):
                split_hi2(n + 3)
                act.wait_ge(xct_done, n + 1)
                if n == 0:
                    act.wait_ge(m_lo, KC)
                act.copy(kp[:, n, :], PS[2 + n % 2][:]).then_inc(xres, 1)
                act.wait_ge(resid, n + 1)
                if n >= 1:
                    act.wait_ge(acc_ok, n + 1)
                act.activation(tmp[:, 1, :], kp[:, n, :], ACT.Square).then_inc(sq_ok, 1)
            act.wait_ge(mean_done, 1)
            act.wait_ge(acc_ok, KC + 1)
            act.activation(tmp[:, 1, :], PS[0][:], ACT.Sqrt, bias=eps_c[:]).then_inc(mean_out, 1)
            act.wait_ge(w_used, CH_OUT + KC)
            for c in range(KC):
                act.activation(hspl[:, 0, c, :], kp[:, c, :], ACT.Copy, scale=gm_g[:, c:c + 1]).then_inc(h_hi, 1)

            def mlp_block(b, last):
                for j in range(4):
                    split_hi2(KC + j + 3, b)
                    act.wait_ge(u_r, b * 4 + (j + 1) + PRIME)
                    act.wait_ge(u_lo, b * 4 + j + PRIME)
                    act.wait_ge(rstd_ok, 1)
                    act.activation(tmp[:, 1, :], tmp[:, 0, :], ACT.Square).then_inc(u_sq, 1)
                    act.wait_ge(u_sq, b * 4 + (j + 1) + PRIME)
                    act.wait_ge(w_used, b * 8 + (CH_OUT + KC))
                    act.copy(hid[:, 0, j, :], tmp[:, 1, :]).then_inc(u_hi, 1)
                for j in range(4, 8):
                    if not last or j + 3 < 8:
                        split_hi2(KC + j + 3, b)
                    if last:
                        if j == 4:
                            act.wait_ge(u_sq, FF_BLOCKS * 4 + PRIME)
                        for m in (2 * j - 8, 2 * j - 7):
                            act.wait_ge(dn_add, b * 8 + (m + 1) + PRIME)
                            if m >= 1:
                                act.wait_ge(facc, m)
                            act.activation(tmp[:, 0, :], kp[:, m, :], ACT.Square).then_inc(fsq, 1)

            with act.Fori(0, FF_BLOCKS - 1) as b:
                mlp_block(b, False)
            mlp_block(FF_BLOCKS - 1, True)
            act.wait_ge(fmean_out, 1)
            act.activation(xstat[:], xstat[:], ACT.Sqrt).then_inc(froot, 1)

        @block.vector
        def _(dve):
            for primed in (pt_lo, on_done, stat_ok, gmul, mixed_ok, u_r, u_lo, dn_add):
                dve.sem_inc(primed, 1)
            chain = [0]

            def link(ins):
                chain[0] += 1
                ins.then_inc(dchain, 1)
                dve.wait_ge(dchain, chain[0])

            def split_lo(slot, chunk):
                dve.wait_ge(w_hi, chunk + 1)
                dve.tensor_tensor(wsp[:, slot, 1, :], raw[:, slot, :], wsp[:, slot, 0, :].bitcast(F32),
                                  ALU.subtract).then_inc(w_lo, 1)

            for half in range(2):
                h4 = slice(4 * half, 4 * half + 4)
                dve.wait_ge(x_sq, 4 * half + 4)
                dve.tensor_scalar(xstat[:, h4], xstat[:, h4], 1.0 / D, EPS, ALU.mult, ALU.add).then_inc(x_st, 1)
                dve.wait_ge(x_root, half + 1)
                dve.reciprocal(xrstd[:, h4], xstat[:, h4]).then_inc(x_rs, 1)
                dve.wait_ge(x_rs, half + 1)
                for i in range(4):
                    t = 4 * half + i
                    dve.tensor_scalar(tmp[:, i, :], tmp[:, i, :], xrstd[:, t:t + 1], None, ALU.mult).then_inc(x_scaled, 1)
                if half == 0:
                    split_lo(2, 0)
                else:
                    split_lo(0, 1)
                    split_lo(1, 2)
                for c in range(KC):
                    n = half * KC + c
                    dve.wait_ge(xhi, n + 1)
                    bank = PS[(n % 4) // 2][:, (n % 2) * HALF:(n % 2 + 1) * HALF]
                    cols = slice(half * HALF, (half + 1) * HALF)
                    dve.scalar_tensor_tensor(out=hspl[:, 1, c, cols], in0=bank, scalar=ga_g[:, c:c + 1],
                                             in1=hspl[:, 0, c, cols].bitcast(F32), op0=ALU.mult,
                                             op1=ALU.subtract).then_inc(xlo, 1)
            H8 = FOX_HEADS
            fz, fe, fc, fo = (tmp[0:H8, i, :] for i in range(4))
            mid = tmp[0:H8, 1, 0:512].bitcast(BF16)
            dve.wait_ge(w_used, 1)
            dve.wait_ge(xt_done, 16)
            dve.wait_ge(small_in, 48)
            dve.tensor_scalar(fz, PS[0][0:H8, :], bfor[0:H8, :], None, ALU.add).then_inc(fz_ok, 1)
            link(dve.memset(fo, 1.0))
            dve.wait_ge(fln_ok, 1)
            dve.wait_ge(fz_ok, 1)
            link(dve.scalar_tensor_tensor(out=fz, in0=fz, scalar=0.0, in1=fe, op0=ALU.min, op1=ALU.subtract))
            link(dve.tensor_tensor_scan(fc, fo, fz, 0.0, ALU.mult, ALU.add))
            dve.wait_ge(consts, N_CONST)
            link(dve.tensor_scalar(fbias[0:H8, :], fc, -1.0, None, ALU.mult))
            link(dve.scalar_tensor_tensor(out=fz, in0=fc, scalar=-1.0, in1=fbias[0:H8, :], op0=ALU.mult,
                                          op1=ALU.subtract))
            link(dve.tensor_copy(mid, fz))
            dve.tensor_copy(fbias[32:32 + H8, :], fz)
            link(dve.tensor_tensor(fz, fz, mid, ALU.subtract))
            dve.tensor_copy(fbias[64:64 + H8, :], fz).then_inc(fbias_ok, 1)
            split_lo(2, 3)
            dve.wait_ge(fbias_ok, 1)

            def attention(dil, t, ub):
                perm = (lambda ap: ap) if dil in (None, 1) else (lambda ap: ap.rearrange("p (l r) -> p r l", r=dil))
                view = (lambda ap: ap) if dil in (None, 1) else (lambda ap: ap.rearrange("p (r l) -> p r l", r=dil))
                for j in range(2):
                    if dil is not None:
                        dve.wait_ge(w_used, t * 3 + (CH0 + j + 1))
                        if j == 0:
                            dve.wait_ge(tr_done, ub + PRIME)
                            dve.wait_ge(rope_in, 16)
                        else:
                            dve.wait_ge(st_lo, t * 6 + 4)
                        a, o = tmp[:, 1 - j, :], tmp[:, j, :]
                        swap = list(range(8, 16)) + list(range(8)) + list(range(16, 32))
                        dve.tensor_tensor(o, PS[j][:], tmp[:, 2, :], ALU.mult).then_inc(roped, 1)
                        dve.stream_shuffle(a, PS[j][:], swap).then_inc(roped, 1)
                        dve.wait_ge(roped, t * 6 + 3 * j + 2)
                        dve.tensor_tensor(a, a, tmp[:, 3, :], ALU.mult).then_inc(roped, 1)
                        dve.wait_ge(roped, t * 6 + 3 * j + 3)
                        dve.tensor_tensor(o, o, a, ALU.add).then_inc(raw_out, 1)
                        dve.wait_ge(raw_out, t * 3 + j + 1)
                    if j == 0:
                        parts = [(q_lo[0][0:64], q_hi[0][0:64], 0), (q_lo[0][64:P], q_hi[0][0:64], 0),
                                 (q_lo[1][64:P], q_hi[1][64:P], 64), (q_lo[1][0:64], q_hi[1][64:P], 64)]
                        dve.wait_ge(st_hi, t * 6 + 4)
                    else:
                        parts = [(k_st[0][64:P], k_st[0][0:64], 0), (k_st[1][0:64], k_st[1][64:P], 64)]
                        dve.wait_ge(st_hi, t * 6 + 6)
                    for dst, hi, row in parts:
                        dve.scalar_tensor_tensor(out=view(dst), in0=perm(tmp[row:row + 64, j, :]),
                                                 scalar=QSCALE if j == 0 else 1.0, in1=view(hi.bitcast(F32)),
                                                 op0=ALU.mult, op1=ALU.subtract).then_inc(st_lo, 1)
                for bank in range(2):
                    dve.wait_ge(v_hi, t * 2 + bank + 1)
                    dve.tensor_tensor(v_nat[:, 4 * bank:4 * bank + 4, :, 1, :],
                                      PS[2][:, bank * HALF:(bank + 1) * HALF].rearrange("p (t h d) -> p t h d", t=4, h=2),
                                      v_nat[:, 4 * bank:4 * bank + 4, :, 0, :].bitcast(F32),
                                      ALU.subtract).then_inc(v_lo, 1)

                def maxes(s):
                    n = len(key_tiles(dil, s // 2))
                    dve.wait_ge(qk_done, t * STEPS + s + 1 + PRIME)
                    dve.tensor_reduce(negmax[:, s:s + 1], PS[s % 2][:, 0:n * P], AX_X, ALU.max,
                                      negate=True).then_inc(max_done, 1)

                def probs_lo(s):
                    for n, (a, b) in enumerate(units_of(dil, s)):
                        u = units_before(dil, s) + n
                        dve.wait_ge(pt_hi, ub + (u + 1))
                        dve.tensor_tensor(pt[:, s % 2, 1, a * P:b * P],
                                          PS[2][:, (u % 2) * HALF:(u % 2) * HALF + (b - a) * P],
                                          pt[:, s % 2, 0, a * P:b * P].bitcast(F32), ALU.subtract).then_inc(pt_lo, 1)

                def inverses(s):
                    dve.wait_ge(exp_done, t * STEPS + s + 1 + PRIME)
                    dve.reciprocal(rowinv[:, s:s + 1], rowsum[:, s:s + 1]).then_inc(inv_done, 1)

                def outs(s):
                    i, h = divmod(s, 2)
                    dve.wait_ge(op_done, t * STEPS + s + 1)
                    dve.wait_ge(inv_done, t * STEPS + s + 1)
                    if i >= 2:
                        dve.wait_ge(ot_done, t * 8 + (i - 1))
                    dve.scalar_tensor_tensor(out=o_nat[:, i % 2, h * HD:(h + 1) * HD],
                                             in0=PS[3][:, h * HALF:h * HALF + HD], scalar=rowinv[:, s:s + 1],
                                             in1=o_part[:, h, :], op0=ALU.mult, op1=ALU.add).then_inc(on_done, 1)

                for s in range(STEPS + 2):
                    if s < STEPS:
                        maxes(s)
                    if 1 <= s <= STEPS:
                        probs_lo(s - 1)
                        inverses(s - 1)
                    if 2 <= s < STEPS + 2:
                        outs(s - 2)
                    if s in (3, 8, 12):
                        j = (3, 8, 12).index(s)
                        split_lo(j, t * 3 + (CH0 + 3 + j))
                if dil is not None:
                    g = DILATIONS.index(dil)
                    pair = t - 2 * g
                    dve.wait_ge(max_done, t * STEPS + STEPS)
                    for dst, src in ((st_nm, negmax), (st_rs, rowsum)):
                        d4 = dst[:, g, :, :, :].rearrange("p i a h -> p i (a h)")
                        ins = dve.tensor_copy(d4[:, :, bass.ds(pair * 2, 2)],
                                              src[:].rearrange("p (i h) -> p i h", h=2))
                    ins.then_inc(stat_ok, 1)

            for g, dil in enumerate(DILATIONS):
                with dve.Fori(0, 2) as pair:
                    attention(dil, pair + 2 * g, (pair + 2 * g) * 16)

            dve.wait_ge(ln_ok, 1)
            dve.wait_ge(stat_ok, N_DIL + PRIME)
            dve.tensor_tensor(st_rs[:], st_rs[:], st_nm[:], ALU.subtract).then_inc(lse_ok, 1)
            for g, dil in enumerate(DILATIONS):
                dve.wait_ge(lt_done, g + 1)
                if g == 0:
                    dve.wait_ge(tr_done, 16 * N_DIL + PRIME)
                dst, src = tmp[0:4, g, :], PS[2 + g % 2][0:4, :]
                if dil > 1:
                    dst = dst.rearrange("p (l r) -> p r l", r=dil)
                    src = src.rearrange("p (r l) -> p r l", r=dil)
                dve.tensor_copy(dst, src).then_inc(lt_out, 1)
            dve.wait_ge(lt_out, 3)
            top = tmp[0:4, 3, :]
            link(dve.tensor_tensor(top, tmp[0:4, 0, :], tmp[0:4, 1, :], ALU.max))
            link(dve.tensor_tensor(top, top, tmp[0:4, 2, :], ALU.max))
            for g in range(3):
                ins = dve.tensor_tensor(tmp[0:4, g, :], tmp[0:4, g, :], top, ALU.subtract)
            ins.then_inc(lsub_ok, 1)
            dve.wait_ge(lexp_ok, 1)
            link(dve.tensor_tensor(top, tmp[0:4, 0, :], tmp[0:4, 1, :], ALU.add))
            link(dve.tensor_tensor(top, top, tmp[0:4, 2, :], ALU.add))
            link(dve.reciprocal(top, top))
            for g in range(3):
                ins = dve.tensor_tensor(tmp[0:4, g, :], tmp[0:4, g, :], top, ALU.mult)
            ins.then_inc(alpha_f, 1)
            dve.wait_ge(alpha_f, 1)
            dve.wait_ge(alpha_hi, 1)
            dve.tensor_tensor(alpha_st[32:36], tmp[0:4, 0:3, :], alpha_st[0:4].bitcast(F32),
                              ALU.subtract).then_inc(alpha_ok, 1)
            dve.wait_ge(ote_done, 8 * N_DIL + PRIME)
            for n in range(6):
                pair, g = divmod(n, 3)
                dve.wait_ge(spr_done, n + 1)
                dst = ob[:, pair * 1024:(pair + 1) * 1024]
                one = dst if g == 0 else tmp[:, 3, :]
                dve.tensor_tensor(one, PS[n % 2][:], og[:, g, pair * 1024:(pair + 1) * 1024], ALU.mult).then_inc(spr_out, 1)
                dve.wait_ge(spr_out, n + 1)
                if g > 0:
                    ins = dve.tensor_tensor(dst, dst, one, ALU.add)
                    if n < 5:
                        link(ins)
                    else:
                        ins.then_inc(comb_ok, 1)
            with dve.Fori(0, N_FOX) as it:
                attention(None, it + N_DIL, it * 24 + 16 * N_DIL)

            T0 = N_DIL + N_FOX
            for k in range(6):
                src = keep[:, k * 1024:(k + 1) * 1024] if k < 4 else ob[:, (k - 4) * 1024:(k - 3) * 1024]
                dve.wait_ge(br_hi, k + 1)
                dve.tensor_tensor(br_in[:, 1, k, :], src, br_in[:, 0, k, :].bitcast(F32), ALU.subtract).then_inc(br_lo, 1)
            with dve.Fori(0, N_GATE) as it:
                for j in range(3):
                    split_lo(j, it * 3 + (CH0 + 3 * T0 + 3 + j))
                dve.wait_ge(w_used, it * 3 + (CH0 + 3 * T0 + 3))
                for j in range(2):
                    dve.wait_ge(sig_ok, it * 2 + (j + 1) + PRIME)
                    dve.tensor_tensor(tmp[:, j, :], tmp[:, j, :], PS[2 + j][:], ALU.mult).then_inc(gmul, 1)
                dve.wait_ge(gmul, it * 2 + 2 + PRIME)
                dve.tensor_tensor(keep[:, bass.ds(it * 1024, 1024)], tmp[:, 0, :], tmp[:, 1, :],
                                  ALU.add).then_inc(mixed_ok, 1)

            dve.wait_ge(mixed_ok, N_GATE + PRIME)
            for c in range(KC):
                dve.wait_ge(m_hi, c + 1)
                dve.tensor_tensor(hspl[:, 1, c, :], kp[:, c, :], hspl[:, 0, c, :].bitcast(F32), ALU.subtract).then_inc(m_lo, 1)

            def split_lo2(n, b=0):
                dve.wait_ge(w_hi, b * 8 + (CH_OUT + n + 1))
                dve.tensor_tensor(wsp_at(n, 1), raw_at(n), wsp_at(n, 0).bitcast(F32), ALU.subtract).then_inc(w_lo, 1)

            dve.memset(tmp[:, 3, :], 0.0).then_inc(acc_ok, 1)
            for n in range(KC):
                split_lo2(n + 3)
                dve.wait_ge(w_used, CH_OUT + n + 1)
                dve.wait_ge(xres, n + 1)
                dve.tensor_tensor(kp[:, n, :], kp[:, n, :], PS[n % 2][:], ALU.add).then_inc(resid, 1)
                dve.wait_ge(sq_ok, n + 1)
                dve.wait_ge(acc_ok, n + 1)
                dve.tensor_tensor(tmp[:, 3, :], tmp[:, 3, :], tmp[:, 1, :], ALU.add).then_inc(acc_ok, 1)
            for c in range(KC):
                dve.wait_ge(h_hi, c + 1)
                dve.scalar_tensor_tensor(out=hspl[:, 1, c, :], in0=kp[:, c, :], scalar=gm_g[:, c:c + 1],
                                         in1=hspl[:, 0, c, :].bitcast(F32), op0=ALU.mult,
                                         op1=ALU.subtract).then_inc(h_lo, 1)
            dve.wait_ge(mean_out, 1)
            dve.reciprocal(tmp[:, 3, :], tmp[:, 1, :]).then_inc(rstd_ok, 1)
            dve.wait_ge(rstd_ok, 1)

            def mlp_block(b, last):
                for j in range(4):
                    split_lo2(KC + j + 3, b)
                    dve.wait_ge(w_used, b * 8 + (CH_OUT + KC + j + 1))
                    dve.wait_ge(u_sq, b * 4 + j + PRIME)
                    dve.scalar_tensor_tensor(out=tmp[:, 0, :], in0=PS[j % 2][:], scalar=0.0, in1=tmp[:, 3, :],
                                             op0=ALU.max, op1=ALU.mult).then_inc(u_r, 1)
                    dve.wait_ge(u_hi, b * 4 + (j + 1))
                    dve.tensor_tensor(hid[:, 1, j, :], tmp[:, 1, :], hid[:, 0, j, :].bitcast(F32),
                                      ALU.subtract).then_inc(u_lo, 1)
                if last:
                    link(dve.memset(tmp[:, 3, :], 0.0))
                for j in range(4, 8):
                    if not last or j + 3 < 8:
                        split_lo2(KC + j + 3, b)
                    for m in (2 * j - 8, 2 * j - 7):
                        if m % 2:
                            dve.wait_ge(w_used, b * 8 + (CH_OUT + KC + 4 + m // 2 + 1))
                        else:
                            dve.wait_ge(dn_even, b * 4 + (m // 2 + 1))
                        dve.tensor_tensor(kp[:, m, :], kp[:, m, :], PS[2 + m % 2][:], ALU.add).then_inc(dn_add, 1)
                        if last:
                            dve.wait_ge(fsq, m + 1)
                            if m:
                                dve.wait_ge(facc, m)
                            dve.tensor_tensor(tmp[:, 3, :], tmp[:, 3, :], tmp[:, 0, :], ALU.add).then_inc(facc, 1)

            with dve.Fori(0, FF_BLOCKS - 1) as b:
                mlp_block(b, False)
            mlp_block(FF_BLOCKS - 1, True)
            dve.wait_ge(fmean, 1)
            dve.tensor_scalar(xstat[:], PS[0][:, 0:8], EPS, None, ALU.add).then_inc(fmean_out, 1)
            dve.wait_ge(froot, 1)
            dve.reciprocal(xrstd[:], xstat[:]).then_inc(frstd, 1)
            dve.wait_ge(frstd, 1)
            dve.wait_ge(gfin_in, 16)
            for i in range(8):
                dve.wait_ge(ft_done, i + 1)
                if i >= 2:
                    dve.wait_ge(y_out[i % 2], 16 * (i // 2))
                dve.scalar_tensor_tensor(out=tmp[:, i % 2, :], in0=PS[1 + i % 3][:], scalar=xrstd[:, i:i + 1],
                                         in1=tmp[:, 2, :], op0=ALU.mult, op1=ALU.mult).then_inc(y_ok, 1)


def kernel(**inputs):
    import numpy as np
    import concourse.bacc as bacc
    from concourse.bass_utils import run_bass_kernel_spmd

    f = {k: np.asarray(v) for k, v in inputs.items()}
    half = HD // 8
    inv = np.power(np.float32(500000.0), -np.arange(half, dtype=np.float32) * np.float32(2.0) / np.float32(2 * half))
    ang = np.arange(S, dtype=np.float32)[None, :] * inv.astype(np.float32)[:, None]
    rope = np.zeros((P, 2, S), np.float32)
    rope[:, 0] = 1.0
    for h in range(2):
        for part in range(2):
            rows = slice(h * HD + part * half, h * HD + (part + 1) * half)
            rope[rows, 0] = np.cos(ang)
            rope[rows, 1] = np.sin(ang) * (1.0 if part else -1.0)
    arrays = {
        "x": np.ascontiguousarray(f["x"][0]),
        "g_attn": np.ascontiguousarray(f["norm_attn_g"][0].reshape(KC, P).T),
        "w_in": np.ascontiguousarray(f["w_in"][0]),
        "b_forget": np.ascontiguousarray(f["b_forget"][0].reshape(FOX_HEADS, 1)),
        "w_branch": np.concatenate([f["w_branch_a"][0], f["w_branch_b"][0]], axis=0),
        "w_out": np.ascontiguousarray(f["w_out"][0]),
        "g_mlp": np.ascontiguousarray(f["norm_mlp_g"][0].reshape(KC, P).T),
        "w_up": np.ascontiguousarray(f["w_up"][0]),
        "w_down": np.ascontiguousarray(f["w_down"][0]),
        "g_final": np.ascontiguousarray(np.broadcast_to(f["norm_final_g"], (P, D))),
        "rope": rope,
    }
    nc = bacc.Bacc("TRN2", target_bir_lowering=False, num_devices=1)
    args = [nc.dram_tensor(f"in_{k}", a.shape, mybir.dt.from_np(a.dtype), kind="ExternalInput").ap()
            for k, a in arrays.items()]
    out = nc.dram_tensor("out_y", (S, D), F32, kind="ExternalOutput").ap()
    build(nc, *args, out)
    r = run_bass_kernel_spmd(nc, [{f"in_{k}": a for k, a in arrays.items()}], core_ids=[0])
    return r.results[0]["out_y"].reshape(1, S, D)
```

```python
from contextlib import ExitStack

import concourse.bass as bass
from concourse import mybir

ALU = mybir.AluOpType
ACT = mybir.ActivationFunctionType
BF16 = mybir.dt.bfloat16
F32 = mybir.dt.float32
F32R = mybir.dt.float32r
AX_X = mybir.AxisListType.X

P = 128
D = 1024
S = 1024
KC = D // P
HD = 64
HALF = 512
EPS = 1e-6
NEG = -1e30
FOX_HEADS = 8
FOX_W = FOX_HEADS * HD
DILATIONS = (1, 4, 16)
DIL_W = 4 * HD * len(DILATIONS)
COL_FA = 3 * FOX_W
COL_QB = COL_FA + FOX_HEADS
COL_KB = COL_QB + DIL_W
COL_VB = COL_KB + DIL_W
COL_GA = COL_VB + DIL_W
COL_GB = COL_GA + D
QSCALE = float(HD) ** -0.5
FF_BLOCKS = 8
N_DIL = 2 * len(DILATIONS)
N_FOX = FOX_HEADS // 2
N_GATE = KC
CH0 = 1
CH_OUT = CH0 + 3 * (N_DIL + N_FOX + N_GATE)
PRIME = 1
STEPS = 16
MIX = N_DIL + N_FOX
def group_steps(t):
    if t == N_DIL:
        return (), (), (2, 3, 4, 5), (6, 7, 8, 9), (10, 11, 12), (13, 14, 15)
    return (0, 1, 2), (3, 4, 5), (6, 7, 8), (9, 10, 11), (12, 13), (14, 15)


def group_out(t, s):
    return next((g for g, steps in enumerate(group_steps(t)) if s - 1 in steps[-1:]), None)


ROTATE_OPS = {3: (0,), 4: (1,), 5: (2, 3), 6: (4, 5), 7: (6, 7), 9: (8,), 10: (9,), 11: (10, 11),
              12: (12, 13), 13: (14, 15)}


def dil_of(t):
    return DILATIONS[t // 2] if t < N_DIL else None


def column(G):
    t, s = divmod(G, STEPS)
    if t >= N_DIL:
        return G
    return (((t // 2) * 8 + s // 2) * 2 + t % 2) * 2 + s % 2


def key_tiles(t, i):
    dil = dil_of(t)
    if dil is None:
        return [(j, "causal" if j == i else None) for j in range(i + 1)]
    if dil == 16:
        return [(i, "twoblock")]
    if i % (8 // dil) == 0:
        return [(i, "causal")]
    return [(i - 1, "prev"), (i, "causal")]


def tiles_of(G):
    return key_tiles(G // STEPS, G % STEPS // 2)


def units_of(G):
    n = len(tiles_of(G))
    return [(a, min(a + 4, n)) for a in range(0, n, 4)]


def units_before(G):
    return sum(len(units_of(x)) for x in range(G))


def tile_tokens(ap, t, i):
    d = dil_of(t)
    if d in (None, 1):
        return ap[:, i * P:(i + 1) * P]
    v = ap.rearrange("p (l r) -> p r l", r=d)
    if d == 4:
        return v[:, i // 2, (i % 2) * P:(i % 2 + 1) * P]
    return v[:, 2 * i:2 * i + 2, :]


def tile_view(ap, t):
    return ap.rearrange("p (r l) -> p r l", r=2) if dil_of(t) == 16 else ap


def natural(ap, t):
    d = dil_of(t)
    return ap if d in (None, 1) else ap.rearrange("p (l r) -> p r l", r=d)


def ordered(ap, t):
    d = dil_of(t)
    return ap if d in (None, 1) else ap.rearrange("p (r l) -> p r l", r=d)


def after(eng, sem, n):
    if n > 0:
        eng.wait_ge(sem, n)


def build(nc, x, g_attn, w_in, b_forget, w_branch, w_out, g_mlp, w_up, w_down, g_final, rope, out):
    w_in_v = w_in.rearrange("(k p) n -> p k n", p=P)
    w_br_v = w_branch.rearrange("(k p) n -> p k n", p=P)
    w_out_v = w_out.rearrange("(k p) n -> p k n", p=P)
    w_up_v = w_up.rearrange("(k p) n -> p k n", p=P)
    w_dn_v = w_down.rearrange("(f p) n -> p f n", p=P)
    x_t = x.rearrange("(t p) d -> p t d", p=P)
    out_t = out.rearrange("(t p) d -> p t d", p=P)

    with ExitStack() as ctx:
        def sb(name, shape, dt):
            return ctx.enter_context(nc.sbuf_tensor(name, shape, dt))

        def sem(name):
            return ctx.enter_context(nc.semaphore(name))

        hspl = sb("hspl", [P, 2, KC, S], F32R)
        work = sb("work", [P, 12 * 1024], F32R)
        keep = sb("keep", [P, 8 * 1024], F32)
        raw = sb("raw", [P, 2, 1024], F32)
        wsp = sb("wsp", [P, 2, 2, 1024], F32R)
        tmp = sb("tmp", [P, 7, 1024], F32)
        fbias = sb("fbias", [P, S], BF16)
        fsel = sb("fsel", [P, FOX_HEADS, P], BF16)
        ident = sb("ident", [P, P], F32)
        ident_b = sb("ident_b", [P, P], BF16)
        masks = sb("masks", [P, 3, P], BF16)
        mean_w = sb("mean_w", [P, P], F32)
        spread_f = sb("spread_f", [P, 2, P], F32)
        spread = sb("spread", [P, 2, P], F32R)
        o_nat = sb("o_nat", [P, 2, P], F32)
        o_part = sb("o_part", [P, 2, HD], F32)
        negmax = sb("negmax", [P, STEPS * MIX], F32)
        rowsum = sb("rowsum", [P, STEPS * MIX], F32)
        rowinv = sb("rowinv", [P, STEPS * MIX], F32)
        xstat = sb("xstat", [P, KC], F32)
        xrstd = sb("xrstd", [P, KC], F32)
        ga_g = sb("ga_g", [P, KC], F32)
        gm_g = sb("gm_g", [P, KC], F32)
        eps_c = sb("eps_c", [P, 1], F32)
        bfor = sb("bfor", [P, 1], F32)
        PS = [ctx.enter_context(nc.psum_tensor(f"ps{i}", [P, 1024], F32)) for i in range(4)]
        MASK = {"causal": masks[:, 0, :], "prev": masks[:, 1, :], "twoblock": masks[:, 2, :]}

        k_st = [[work[:, (2 * b + h) * 1024:(2 * b + h + 1) * 1024] for h in range(2)] for b in range(2)]
        v_nat = work[:, 4 * 1024:6 * 1024].rearrange("p (t h s d) -> p t h s d", t=8, h=2, s=2)
        q_st = work[:, 6144:6912].rearrange("p (b s c) -> p b s c", b=3, s=2)
        pt = work[:, 8 * 1024:12 * 1024].rearrange("p (b s c) -> p b s c", b=2, s=2)
        alpha_nat = work[:, 11264:11456].rearrange("p (g i s h) -> p g i s h", g=3, i=8, s=2)
        alpha_st = work[0:8, 8192:8192 + 3072].rearrange("p (g c) -> p g c", g=3)
        k_raw, v_raw = tmp[:, 4, :], tmp[:, 5, :]
        rope_c, rope_s = tmp[:, 0, :], tmp[:, 1, :]
        psc = [PS[0], PS[1]]

        def psp(u, g):
            return (PS[0] if u <= N_DIL and g % 2 else PS[3])[:, HALF:2 * HALF]

        pso = PS[3][:, 0:HALF]
        lse_nat = tmp[:, 6, 0:96].rearrange("p (g c) -> p g c", g=3)
        top = tmp[:, 6, 96:128]
        lrow = [tmp[0:4, 0, :], tmp[0:4, 1, :], tmp[0:4, 3, :]]

        def q_raw(t):
            return tmp[:, 2 + t % 2, :]

        def probs(G):
            if G < STEPS * N_DIL:
                return tmp[:, 6, (G % 2) * 256:(G % 2 + 1) * 256]
            return tmp[:, G % 2, :]

        br_in = work[:, :].rearrange("p (s k c) -> p s k c", s=2, k=6)
        hid = work[:, 0:8192].rearrange("p (s f c) -> p s f c", s=2, f=4)

        og = keep[:, 0:6144].rearrange("p (g c) -> p g c", g=3)
        ob = keep[:, 6144:8192]
        kp = keep[:, :].rearrange("p (k c) -> p k c", k=KC)

        def raw_at(n):
            return (raw[:, 1, :], raw[:, 0, :], tmp[:, 2, :], tmp[:, 4, :])[n % 4]

        def wsp_at(n, part):
            return (wsp[:, 1, part, :], wsp[:, 0, part, :], work[:, 8192 + part * 1024:9216 + part * 1024],
                    work[:, 10240 + part * 1024:11264 + part * 1024])[n % 4]

        def loaded_at(n):
            return ((w_in_s[1], 28 + n // 4), (w_in_s[0], 29 + n // 4), (w_in_s[2], 1 + n // 4),
                    (w_in_s[3], 1 + n // 4))[n % 4]

        def to_natural(g, copy, eng):
            eng.wait_ge(lt_done, g + 1)
            dst, src, dil = lrow[g], PS[g][0:4, :], DILATIONS[g]
            if dil > 1:
                dst = dst.rearrange("p (l r) -> p r l", r=dil)
                src = src.rearrange("p (r l) -> p r l", r=dil)
            copy(dst, src).then_inc(lt_out[g], 1)

        x_in = [sem(f"x_in{i}") for i in range(4)]
        small_in = sem("small_in")
        rope_in = sem("rope_in")
        xcol_in = sem("xcol_in")
        gfin_in = sem("gfin_in")
        w_in_s = [sem(f"w_loaded{i}") for i in range(4)]
        w_hi = sem("w_hi")
        w_lo = sem("w_lo")
        w_used = sem("w_used")
        consts = sem("consts")
        fsel_ok = sem("fsel_ok")
        spread_ok = sem("spread_ok")
        x_sq = sem("x_sq")
        x_st = sem("x_st")
        x_root = sem("x_root")
        x_rs = sem("x_rs")
        x_scaled = sem("x_scaled")
        xt_done = sem("xt_done")
        xhi = sem("xhi")
        xlo = sem("xlo")
        dchain = sem("dchain")
        achain = sem("achain")
        fz_ok = sem("fz_ok")
        fln_ok = sem("fln_ok")
        fbias_ok = sem("fbias_ok")
        raw_out = sem("raw_out")
        roped = sem("roped")
        half_done = sem("half_done")
        k_hi = sem("k_hi")
        k_lo = sem("k_lo")
        q_hi = sem("q_hi")
        q_lo = sem("q_lo")
        vt_done = sem("vt_done")
        v_hi = sem("v_hi")
        v_lo = sem("v_lo")
        qk_done = sem("qk_done")
        max_done = sem("max_done")
        exp_done = sem("exp_done")
        inv_done = sem("inv_done")
        tr_done = sem("tr_done")
        pt_hi = sem("pt_hi")
        pt_lo = sem("pt_lo")
        pv_done = sem("pv_done")
        op_done = sem("op_done")
        on_done = sem("on_done")
        ot_done = sem("ot_done")
        ote_done = sem("ote_done")
        ln_ok = sem("ln_ok")
        lse_ok = sem("lse_ok")
        lt_done = sem("lt_done")
        lt_out = [sem(f"lt_out{g}") for g in range(3)]
        ln_done = sem("ln_done")
        lsub_ok = sem("lsub_ok")
        lexp_ok = sem("lexp_ok")
        alpha_f = sem("alpha_f")
        alpha_hi = sem("alpha_hi")
        alpha_lo = sem("alpha_lo")
        at_done = sem("at_done")
        alpha_row = [sem(f"alpha_row{g}") for g in range(3)]
        spr_done = sem("spr_done")
        spr_out = sem("spr_out")
        comb_ok = sem("comb_ok")
        br_hi = sem("br_hi")
        br_lo = sem("br_lo")
        sig_ok = sem("sig_ok")
        gmul = sem("gmul")
        mixed_ok = sem("mixed_ok")
        m_hi = sem("m_hi")
        m_lo = sem("m_lo")
        xct_done = sem("xct_done")
        xres = sem("xres")
        resid = sem("resid")
        sq_ok = sem("sq_ok")
        acc_ok = sem("acc_ok")
        mean_done = sem("mean_done")
        mean_out = sem("mean_out")
        rstd_ok = sem("rstd_ok")
        h_hi = sem("h_hi")
        h_lo = sem("h_lo")
        u_r = sem("u_r")
        u_sq = sem("u_sq")
        u_hi = sem("u_hi")
        u_lo = sem("u_lo")
        dn_even = sem("dn_even")
        dn_add = sem("dn_add")
        fsq = sem("fsq")
        facc = sem("facc")
        fmean = sem("fmean")
        fmean_out = sem("fmean_out")
        froot = sem("froot")
        frstd = sem("frstd")
        ft_done = sem("ft_done")
        y_ok = sem("y_ok")
        y_out = [sem(f"y_out{i}") for i in range(2)]

        block = ctx.enter_context(nc.Block())

        @block.sync
        def _(sp):
            def load_chunk(slot, src, dst=None):
                dst = raw[:, slot, :] if dst is None else dst
                n = src.shape[1] * src.shape[2]
                sp.dma_start(dst[:, 0:n].rearrange("p (k c) -> p k c", k=src.shape[1]), src).then_inc(w_in_s[slot], 16)

            for i in range(4):
                sp.dma_start(tmp[:, i, :], x_t[:, i, :]).then_inc(x_in[i], 16)
            sp.dma_start(ga_g[:], g_attn).then_inc(small_in, 16)
            sp.dma_start(gm_g[:], g_mlp).then_inc(small_in, 16)
            sp.dma_start(bfor[0:FOX_HEADS, :], b_forget).then_inc(small_in, 16)
            load_chunk(0, w_in_v[:, :, COL_FA:COL_FA + P])
            load_chunk(1, w_in_v[:, :, COL_KB:COL_KB + P])
            sp.wait_ge(xt_done, 8)
            for i in range(4):
                sp.dma_start(tmp[:, i, :], x_t[:, 4 + i, :]).then_inc(x_in[i], 16)
            for c in range(2, CH_OUT):
                t, j = divmod(c - CH0, 3)
                m = (t if t < N_DIL else t - N_DIL if t < MIX else t - MIX) * P
                cols = ((COL_KB, COL_QB, COL_VB) if t < N_DIL else (FOX_W, 0, 2 * FOX_W) if t < MIX
                        else (COL_GA, COL_GB, 0))
                src = w_br_v[:, :, m:m + P] if t >= MIX and j == 2 else w_in_v[:, :, cols[j] + m:cols[j] + m + P]
                sp.wait_ge(w_lo, c - 1)
                load_chunk(c % 2, src)
                if c == 2:
                    sp.wait_ge(fbias_ok, 1)
                    sp.dma_start(tmp[:, 0:2, :], rope).then_inc(rope_in, 16)

            def xcol(m):
                sp.dma_start(tmp[:, 0, :].rearrange("p (t c) -> p t c", t=8),
                             x_t[:, :, bass.ds(m * P, P) if not isinstance(m, int) else slice(m * P, m * P + P)]
                             ).then_inc(xcol_in, 16)

            SLOT = (1, 0, 2, 3)
            for n in range(4):
                sp.wait_ge(w_lo, CH_OUT - 1 + min(n, 1))
                load_chunk(SLOT[n], w_out_v[:, :, n * P:(n + 1) * P], raw_at(n))
            sp.wait_ge(mixed_ok, N_GATE + PRIME)
            xcol(0)
            for n in range(KC):
                if n < KC - 1:
                    sp.wait_ge(xct_done, n + 1)
                    xcol(n + 1)
                if n + 4 < KC:
                    sp.wait_ge(w_lo, CH_OUT + n + 1)
                    load_chunk(SLOT[n % 4], w_out_v[:, :, (n + 4) * P:(n + 5) * P], raw_at(n + 4))
            with sp.Fori(0, FF_BLOCKS) as b:
                for c in range(8):
                    sp.wait_ge(w_lo, b * 8 + (CH_OUT + KC + c - 4 + 1))
                    if c < 4:
                        src = w_up_v[:, :, bass.ds(b * 512 + c * P, P)]
                    else:
                        src = w_dn_v[:, bass.ds(b * 4, 4), (c - 4) * 256:(c - 3) * 256]
                    load_chunk(SLOT[c % 4], src, raw_at(c))
            sp.wait_ge(w_lo, CH_OUT + KC + 8 * FF_BLOCKS)
            sp.dma_start(tmp[:, 2, :], g_final).then_inc(gfin_in, 16)
            for i in range(8):
                sp.wait_ge(y_ok, i + 1)
                sp.dma_start(out_t[:, i, :], tmp[:, i % 2, :]).then_inc(y_out[i % 2], 16)
            for i in range(2):
                sp.wait_ge(y_out[i], 16 * 4)

        @block.gpsimd
        def _(pool):
            n = [0]

            def step(ins):
                n[0] += 1
                ins.then_inc(consts, 1)

            def settle():
                pool.wait_ge(consts, n[0])

            step(pool.memset(ident[:], 0.0))
            step(pool.memset(ident_b[:], 0.0))
            step(pool.memset(masks[:], 0.0))
            step(pool.memset(mean_w[:], 1.0 / D))
            step(pool.memset(eps_c[:], EPS))
            step(pool.memset(fbias[:], 0.0))
            step(pool.memset(fsel[:], 0.0))
            step(pool.memset(spread_f[:], 0.0))
            settle()
            for m in (ident, ident_b):
                step(pool.affine_select(out=m[:], in_=m[:], compare_op=ALU.not_equal, fill=1.0, base=0,
                                        pattern=[[-1, P]], channel_multiplier=1))
            step(pool.affine_select(out=masks[:, 0, :], in_=masks[:, 0, :], compare_op=ALU.is_ge, fill=NEG,
                                    base=0, pattern=[[-1, P]], channel_multiplier=1))
            step(pool.affine_select(out=masks[:, 1, :], in_=masks[:, 1, :], compare_op=ALU.is_ge, fill=NEG,
                                    base=0, pattern=[[1, P]], channel_multiplier=-1))
            step(pool.affine_select(out=masks[:, 2, :], in_=masks[:, 2, :], compare_op=ALU.is_ge, fill=NEG,
                                    base=0, pattern=[[-1, P]], channel_multiplier=1))
            settle()
            step(pool.affine_select(out=masks[:, 2, 0:64], in_=masks[:, 2, 0:64], compare_op=ALU.is_ge, fill=NEG,
                                    base=63, pattern=[[0, 64]], channel_multiplier=-1))
            for r in range(3):
                settle()
                step(pool.affine_select(out=fsel[:], in_=fsel[:], compare_op=ALU.not_equal, fill=1.0, base=-32 * r,
                                        pattern=[[-1, FOX_HEADS], [0, P]], channel_multiplier=1))
            sv = spread_f[:].rearrange("p a (h d) -> p a h d", h=2)
            for r in range(2):
                settle()
                step(pool.affine_select(out=sv, in_=sv, compare_op=ALU.not_equal, fill=1.0, base=-4 * r,
                                        pattern=[[-2, 2], [-1, 2], [0, HD]], channel_multiplier=1))

        N_CONST = 8 + 5 + 1 + 3 + 2

        @block.tensor
        def _(pe):
            def split_products(ps, w, mv, ks, last_inc=None):
                ins = None
                for half in range(2):
                    cols = slice(half * HALF, (half + 1) * HALF)
                    for k in range(ks):
                        for n, (wp, mp) in enumerate(((0, 0), (0, 1), (1, 0))):
                            ins = pe.matmul(ps[:, cols], w(wp, k), mv(mp, k)[:, cols],
                                            start=(k == 0 and n == 0), stop=(k == ks - 1 and n == 2))
                return ins

            def w_of(c):
                return lambda part, k: wsp[:, c % 2, part, k * P:(k + 1) * P]

            def h_at(part, k):
                return hspl[:, part, k, :]

            pe.wait_ge(consts, N_CONST)
            for half in range(2):
                for c in range(KC):
                    n = half * KC + c
                    if c == 0:
                        pe.wait_ge(x_scaled, 4 * half + 4)
                    if n >= 4:
                        pe.wait_ge(xlo, n - 3)
                    bank = PS[(n % 4) // 2][:, (n % 2) * HALF:(n % 2 + 1) * HALF]
                    for t in range(4):
                        ins = pe.transpose(bank[:, t * P:(t + 1) * P], tmp[:, t, c * P:(c + 1) * P], ident[:])
                    ins.then_inc(xt_done, 1)
            pe.wait_ge(xlo, 16)
            pe.wait_ge(w_lo, 1)
            split_products(PS[0], w_of(0), h_at, KC).then_inc(w_used, 1)

            def project(u, g, a, b):
                c = CH0 + 3 * u + g // 2
                cols = slice((g % 2) * HALF, (g % 2 + 1) * HALF)
                if a == 0:
                    after(pe, raw_out, 6 * u + g - (1 if u <= N_DIL and g else 0))
                    pe.wait_ge(w_lo, c + 1)
                for n in range(a, b):
                    k, (wp, mp) = n // 3, ((0, 0), (0, 1), (1, 0))[n % 3]
                    ins = pe.matmul(psp(u, g), wsp[:, c % 2, wp, k * P:(k + 1) * P], hspl[:, mp, k, cols],
                                    start=(n == 0), stop=(n == 23), skip_group_check=True)
                if b == 24:
                    ins.then_inc(w_used if g % 2 else half_done, 1)

            def project_part(G, part):
                t, s = divmod(G, STEPS)
                if t + 1 < MIX:
                    for g, steps in enumerate(group_steps(t)):
                        if s in steps:
                            per = 24 // len(steps)
                            a = (s - steps[0]) * per
                            project(t + 1, g, a + per * part // 3, a + per * (part + 1) // 3)

            def scores(G):
                t, s = divmod(G, STEPS)
                h = s % 2
                tiles = tiles_of(G)
                if s < 2:
                    pe.wait_ge(k_lo, 2 * t + s + 1)
                pe.wait_ge(q_lo, 2 * G + 2)
                after(pe, exp_done, G - 1)
                ps = psc[G % 2]
                base = tiles[0][0]
                end = tiles[-1][0] + 1 - base
                for c0 in range(0, end, 4):
                    n = min(4, end - c0)
                    o = ps[:, c0 * P:(c0 + n) * P]
                    kc = slice((base + c0) * P, (base + c0 + n) * P)
                    ops = [(q_st[:, G % 3, 0, :], k_st[t % 2][h][:, kc], o),
                           (q_st[:, G % 3, 1, :], k_st[t % 2][h][:, kc], o)]
                    if t >= N_DIL:
                        ops.append((fsel[:, 2 * (t - N_DIL) + h, :], fbias[:, kc], o))
                    for j, mask in tiles:
                        if mask and c0 <= j - base < c0 + n:
                            a = (j - base) * P
                            ops.append((ident_b[:], MASK[mask], ps[:, a:a + P]))
                    for m, (lt, rh, oo) in enumerate(ops):
                        ins = pe.matmul(oo, lt, rh, start=(m == 0), stop=(m == len(ops) - 1), skip_group_check=True)
                ins.then_inc(qk_done, 1)

            def transposes(G):
                pe.wait_ge(exp_done, G + 1)
                if G % STEPS == 1:
                    pe.wait_ge(v_lo, 2 * (G // STEPS) + 2)
                for n, (a, b) in enumerate(units_of(G)):
                    u = units_before(G) + n
                    after(pe, pt_lo, u - 1)
                    for k in range(a, b):
                        ins = pe.transpose(PS[2][:, (u % 2) * HALF + (k - a) * P:(u % 2) * HALF + (k - a + 1) * P],
                                           probs(G)[:, k * P:(k + 1) * P], ident[:])
                    ins.then_inc(tr_done, 1)

            def out_transpose(i):
                pe.wait_ge(on_done, 2 * i + 2)
                pe.transpose(pso[:, 256:256 + P], o_nat[:, i % 2, :], ident[:]).then_inc(ot_done, 1)

            def values(G):
                t, s = divmod(G, STEPS)
                tiles = tiles_of(G)
                pe.wait_ge(pt_lo, units_before(G + 1))
                pe.wait_ge(v_lo, 2 * t + 2)
                after(pe, on_done, G)
                after(pe, ote_done, (G - 1) // 2)
                o = pso[:, (s % 2) * P:(s % 2 + 1) * P]
                for part in range(2):
                    for n, (j, _) in enumerate(tiles):
                        ins = pe.matmul(o, pt[:, G % 2, part, n * P:(n + 1) * P],
                                        v_nat[:, j, s % 2, :, :].rearrange("p s d -> p (s d)"),
                                        start=(part == 0 and n == 0), stop=(part == 1 and n == len(tiles) - 1))
                ins.then_inc(pv_done, 1)

            def value_transposes(t):
                pe.wait_ge(raw_out, 6 * t + 6)
                pe.wait_ge(pt_lo, units_before(STEPS * t + 1))
                for i in range(8):
                    ins = pe.transpose(PS[2][:, i * P:(i + 1) * P], v_raw[:, i * P:(i + 1) * P], ident[:])
                    if i % 4 == 3:
                        ins.then_inc(vt_done, 1)

            def mixer_steps(first, last):
                for G in range(first, last + 4):
                    if G < last:
                        scores(G)
                    if G < last:
                        project_part(G, 0)
                    if first <= G - 1 < last:
                        transposes(G - 1)
                    if G < last:
                        project_part(G, 1)
                    if G < last:
                        project_part(G, 2)
                    if G % 2 == 0 and G - 4 >= first:
                        out_transpose((G - 4) // 2)
                    if first <= G - 2 < last:
                        values(G - 2)
                    if G % STEPS == 1 and G < last:
                        value_transposes(G // STEPS)

            project(0, 0, 0, 24)
            pe.wait_ge(fz_ok, 1)
            for g in range(1, 6):
                project(0, g, 0, 24)
            mixer_steps(0, STEPS * N_DIL)

            project(N_DIL + 1, 0, 0, 8)
            pe.wait_ge(lse_ok, 1)
            pe.wait_ge(exp_done, STEPS * N_DIL)
            pe.wait_ge(pt_lo, STEPS * N_DIL)
            lse_v = rowsum[:, 0:96].rearrange("p (g i c) -> p g i c", g=3, i=8)
            for g in range(3):
                for i in range(8):
                    ins = pe.transpose(PS[g][0:4, i * P:(i + 1) * P], lse_v[:, g, i, :], ident[:])
                ins.then_inc(lt_done, 1)
            project(N_DIL + 1, 0, 8, 16)
            pe.wait_ge(ote_done, 8 * N_DIL)
            for g in range(3):
                pe.wait_ge(lt_out[g], 1)
                for i in range(8):
                    ins = pe.transpose(pso[:, g * 32 + i * 4:g * 32 + i * 4 + 4], lrow[g][:, i * P:(i + 1) * P],
                                       ident[0:4, 0:4])
            ins.then_inc(ln_done, 1)
            project(N_DIL + 1, 0, 16, 24)
            pe.wait_ge(alpha_lo, 1)
            for g in range(3):
                for i in range(8):
                    ins = pe.transpose(PS[g][0:8, i * P:(i + 1) * P],
                                       alpha_nat[:, g, i, :, :].rearrange("p s h -> p (s h)").bitcast(F32), ident[:])
                ins.then_inc(at_done, 1)
            pe.wait_ge(spread_ok, 1)
            for n in range(6):
                pair, g = divmod(n, 3)
                if n < 4:
                    project(N_DIL + 1, 1, 6 * n, 6 * n + 6)
                pe.wait_ge(alpha_row[g], 1)
                if n >= 2:
                    pe.wait_ge(spr_out, n - 1)
                for half in range(2):
                    cols = slice(half * HALF, (half + 1) * HALF)
                    ins = pe.matmul(PS[n % 2][:, cols], spread[0:8, pair, :], alpha_st[:, g, cols], start=True, stop=True)
                ins.then_inc(spr_done, 1)
            pe.wait_ge(spr_out, 6)

            mixer_steps(STEPS * N_DIL, STEPS * MIX)

            pe.wait_ge(exp_done, STEPS * MIX)
            pe.wait_ge(pt_lo, units_before(STEPS * MIX))
            pe.wait_ge(ote_done, 8 * MIX)
            with pe.Fori(0, N_GATE // 2) as it:
                for n in range(6):
                    m, j = divmod(n, 3)
                    c = CH0 + 3 * MIX + n
                    if j < 2:
                        pe.wait_ge(sig_ok, it * 4 + 2 * m + PRIME)
                        pe.wait_ge(w_lo, it * 6 + (c + 1))
                        split_products(PS[j], w_of(c), h_at, KC).then_inc(w_used, 1)
                    else:
                        pe.wait_ge(br_lo, 6)
                        pe.wait_ge(gmul, it * 4 + 2 * m + PRIME)
                        pe.wait_ge(w_lo, it * 6 + (c + 1))
                        split_products(PS[2], w_of(c), lambda part, k: br_in[:, part, k, :], 4)
                        split_products(PS[3], lambda part, k, c=c: wsp[:, c % 2, part, (4 + k) * P:(5 + k) * P],
                                       lambda part, k: br_in[:, part, 4 + k, :], 2).then_inc(w_used, 1)

            pe.wait_ge(gmul, 2 * N_GATE + PRIME)
            pe.wait_ge(sig_ok, 2 * N_GATE + PRIME)
            for n in range(KC):
                pe.wait_ge(xcol_in, 16 * (n + 1))
                if n >= 2:
                    pe.wait_ge(xres, n - 1)
                for t in range(8):
                    ins = pe.transpose(PS[2 + n % 2][:, t * P:(t + 1) * P], tmp[:, 0, t * P:(t + 1) * P], ident[:])
                ins.then_inc(xct_done, 1)
                pe.wait_ge(w_lo, CH_OUT + n + 1)
                if n >= 2:
                    pe.wait_ge(resid, n - 1)
                if n == 0:
                    pe.wait_ge(m_lo, KC)
                split_products(PS[n % 2], lambda part, k: wsp_at(n, part)[:, k * P:(k + 1) * P], h_at,
                               KC).then_inc(w_used, 1)

            def mean_square(done):
                for half in range(2):
                    cols = slice(half * HALF, (half + 1) * HALF)
                    ins = pe.matmul(PS[0][:, cols], mean_w[:], tmp[:, 3, cols], start=True, stop=True)
                ins.then_inc(done, 1)

            pe.wait_ge(resid, KC)
            pe.wait_ge(acc_ok, KC + 1)
            mean_square(mean_done)

            with pe.Fori(0, FF_BLOCKS) as b:
                for j in range(4):
                    if j == 0:
                        pe.wait_ge(h_lo, KC)
                        pe.wait_ge(mean_out, 1)
                    if j < 2:
                        pe.wait_ge(u_r, b * 4 + PRIME)
                    else:
                        pe.wait_ge(u_r, b * 4 + (j - 1) + PRIME)
                    pe.wait_ge(w_lo, b * 8 + (CH_OUT + KC + j + 1))
                    split_products(PS[j % 2], lambda part, k: wsp_at(j, part)[:, k * P:(k + 1) * P], h_at,
                                   KC).then_inc(w_used, 1)
                for m, hidden in [(0, (0, 1, 2)), (1, (0, 1, 2)), (0, (3,)), (1, (3,))] + [(m, (0, 1, 2, 3))
                                                                                      for m in range(2, 8)]:
                    if hidden[0] == 0:
                        if m % 2 == 0:
                            pe.wait_ge(w_lo, b * 8 + (CH_OUT + KC + 4 + m // 2 + 1))
                        if m < 2:
                            pe.wait_ge(dn_add, b * 8 + PRIME)
                        else:
                            pe.wait_ge(dn_add, b * 8 + (m - 1) + PRIME)
                    if m == 0:
                        pe.wait_ge(u_lo, b * 4 + (hidden[-1] + 1) + PRIME)
                    for half in range(2):
                        cols = slice(half * HALF, (half + 1) * HALF)
                        for f in hidden:
                            for n, (wp, mp) in enumerate(((0, 0), (0, 1), (1, 0))):
                                a = f * 256 + (m % 2) * P
                                ins = pe.matmul(PS[2 + m % 2][:, cols], wsp_at(m // 2, wp)[:, a:a + P],
                                                hid[:, mp, f, cols], start=(f == 0 and n == 0),
                                                stop=(f == 3 and n == 2), skip_group_check=True)
                    if hidden[-1] == 3:
                        ins.then_inc(w_used if m % 2 else dn_even, 1)

            pe.wait_ge(facc, KC)
            for i in range(8):
                ins = pe.matmul(PS[0][:, i:i + 1], tmp[:, 3, i * P:(i + 1) * P], mean_w[:, 0:1], start=True, stop=True)
            ins.then_inc(fmean, 1)
            for i in range(8):
                if i >= 3:
                    pe.wait_ge(y_ok, i - 2)
                for c in range(KC):
                    ins = pe.transpose(PS[1 + i % 3][:, c * P:(c + 1) * P], kp[:, c, i * P:(i + 1) * P], ident[:])
                ins.then_inc(ft_done, 1)

        @block.scalar
        def _(act):
            for primed in (sig_ok, u_sq):
                act.sem_inc(primed, 1)
            chain = [0]

            def link(ins):
                chain[0] += 1
                ins.then_inc(achain, 1)
                act.wait_ge(achain, chain[0])

            def split_hi(c, wait=0):
                act.wait_ge(w_in_s[c % 2], 16 * (c // 2 + 1))
                after(act, w_used, c - 1)
                act.copy(wsp[:, c % 2, 0, :], raw[:, c % 2, :]).then_inc(w_hi, 1)

            for half in range(2):
                for i in range(4):
                    act.wait_ge(x_in[i], 16 * (half + 1))
                    act.wait_ge(x_sq, 4 * half + i)
                    act.activation(PS[3][:], tmp[:, i, :], ACT.Square,
                                   accum_out=xstat[:, 4 * half + i:4 * half + i + 1]).then_inc(x_sq, 1)
                act.wait_ge(x_st, half + 1)
                act.activation(xstat[:, 4 * half:4 * half + 4], xstat[:, 4 * half:4 * half + 4],
                               ACT.Sqrt).then_inc(x_root, 1)
                if half == 0:
                    act.wait_ge(small_in, 48)
                    split_hi(0)
                else:
                    split_hi(1)
                for c in range(KC):
                    n = half * KC + c
                    act.wait_ge(xt_done, n + 1)
                    bank = PS[(n % 4) // 2][:, (n % 2) * HALF:(n % 2 + 1) * HALF]
                    act.activation(hspl[:, 0, c, half * HALF:(half + 1) * HALF], bank, ACT.Copy,
                                   scale=ga_g[:, c:c + 1]).then_inc(xhi, 1)
            act.wait_ge(consts, N_CONST)
            act.copy(spread[:], spread_f[:]).then_inc(spread_ok, 1)
            act.wait_ge(fz_ok, 1)
            fz, fe = tmp[0:FOX_HEADS, 0, :], tmp[0:FOX_HEADS, 1, :]
            link(act.activation(fe, fz, ACT.Abs))
            link(act.activation(fe, fe, ACT.Exp, scale=-1.0))
            act.activation(fe, fe, ACT.Ln, bias=1.0).then_inc(fln_ok, 1)
            split_hi(2)

            def group_wait(u, g):
                if g % 2:
                    act.wait_ge(w_used, CH0 + 3 * u + g // 2 + 1)
                else:
                    act.wait_ge(half_done, 3 * u + g // 2 + 1)

            def raw_evacuate(u, g):
                group_wait(u, g)
                if g == 0:
                    after(act, k_lo, 2 * u)
                elif g == 2:
                    after(act, q_lo, 2 * STEPS * (u - 1))
                    act.wait_ge(fbias_ok, 1)
                elif g == 4:
                    after(act, vt_done, 2 * u)
                    if u < N_DIL:
                        act.wait_ge(roped, 16 * u + 16)
                half = g % 2
                if g < 4:
                    dst = (k_raw if g < 2 else q_raw(u))[:, half * HALF:(half + 1) * HALF]
                    src = psp(u, g)
                else:
                    d = dil_of(u) or 1
                    n = HALF // d
                    dst = v_raw.rearrange("p (r l) -> p r l", r=d)[:, :, half * n:(half + 1) * n]
                    src = psp(u, g).rearrange("p (l r) -> p r l", r=d)
                act.copy(dst, src).then_inc(raw_out, 1)

            def k_stack(u, h):
                act.wait_ge(raw_out, 6 * u + 2)
                if u < N_DIL:
                    act.wait_ge(roped, 16 * u + 8)
                after(act, qk_done, STEPS * (u - 1))
                row = 64 * h
                act.copy(ordered(k_st[u % 2][h][row:row + 64], u), natural(k_raw[row:row + 64], u)).then_inc(k_hi, 1)

            def q_tile(G):
                t, s = divmod(G, STEPS)
                act.wait_ge(raw_out, 6 * t + 4)
                if t < N_DIL:
                    act.wait_ge(roped, 16 * t + 16)
                after(act, qk_done, G - 2)
                row = 64 * (s % 2)
                for dst in (0, 64):
                    act.activation(tile_view(q_st[dst:dst + 64, G % 3, 0, :], t),
                                   tile_tokens(q_raw(t)[row:row + 64], t, s // 2), ACT.Copy,
                                   scale=QSCALE).then_inc(q_hi, 1)

            def values_hi(t):
                for bank in range(2):
                    act.wait_ge(vt_done, 2 * t + bank + 1)
                    after(act, pv_done, STEPS * t)
                    act.copy(v_nat[:, 4 * bank:4 * bank + 4, :, 0, :],
                             PS[2][:, bank * HALF:(bank + 1) * HALF].rearrange("p (t h d) -> p t h d", t=4, h=2)
                             ).then_inc(v_hi, 1)

            def exps(G):
                n = len(tiles_of(G))
                c = column(G)
                act.wait_ge(max_done, G + 1)
                after(act, tr_done, units_before(G - 1))
                act.activation(probs(G)[:, 0:n * P], psc[G % 2][:, 0:n * P], ACT.Exp,
                               bias=negmax[:, c:c + 1], accum_out=rowsum[:, c:c + 1]).then_inc(exp_done, 1)

            def probs_hi(G):
                for n, (a, b) in enumerate(units_of(G)):
                    u = units_before(G) + n
                    act.wait_ge(tr_done, u + 1)
                    after(act, pv_done, G - 1)
                    act.copy(pt[:, G % 2, 0, a * P:b * P],
                             PS[2][:, (u % 2) * HALF:(u % 2) * HALF + (b - a) * P]).then_inc(pt_hi, 1)

            def out_part(G):
                c = column(G)
                act.wait_ge(pv_done, G + 1)
                act.wait_ge(inv_done, G + 1)
                after(act, on_done, G - 1)
                act.activation(o_part[:, G % 2, :], pso[:, (G % 2) * P + HD:(G % 2 + 1) * P], ACT.Copy,
                               scale=rowinv[:, c:c + 1]).then_inc(op_done, 1)

            def out_store(i):
                act.wait_ge(ot_done, i + 1)
                act.wait_ge(pv_done, min(2 * i + 3, STEPS * (N_DIL if i < 8 * N_DIL else MIX)))
                t, tile = divmod(i, 8)
                if t < N_DIL:
                    dst = tile_tokens(og[:, t // 2, (t % 2) * 1024:(t % 2 + 1) * 1024], t, tile)
                else:
                    dst = keep[:, (t - N_DIL) * 1024 + tile * P:(t - N_DIL) * 1024 + (tile + 1) * P]
                act.copy(dst, tile_view(pso[:, 256:256 + P], t)).then_inc(ote_done, 1)

            def mixer_steps(first, last):
                for G in range(first, last + 4):
                    t, s = divmod(G, STEPS)
                    if group_out(t, s) is not None and G < last and t + 1 < MIX:
                        raw_evacuate(t + 1, group_out(t, s))
                    if s == 0 and G > first and t < MIX:
                        raw_evacuate(t, 5)
                    if G % 2 and G - 5 >= first:
                        out_store((G - 5) // 2)
                    if first <= G - 3 < last:
                        out_part(G - 3)
                    if G < last and G + 2 < STEPS * MIX:
                        q_tile(G + 2)
                    if G < last:
                        exps(G)
                    if first <= G - 1 < last:
                        probs_hi(G - 1)
                    if G < last:
                        if s == 1:
                            values_hi(t)
                        if s == (0 if t == N_DIL else 2):
                            split_hi(CH0 + 3 * t + 4)
                        if t + 1 < MIX:
                            if s == 7:
                                split_hi(CH0 + 3 * t + 5)
                            if s in (8, 9):
                                k_stack(t + 1, s - 8)
                            if s == 13:
                                split_hi(CH0 + 3 * t + 6)

            raw_evacuate(0, 0)
            raw_evacuate(0, 1)
            split_hi(3)
            k_stack(0, 0)
            k_stack(0, 1)
            raw_evacuate(0, 2)
            raw_evacuate(0, 3)
            split_hi(4)
            q_tile(0)
            q_tile(1)
            raw_evacuate(0, 4)
            raw_evacuate(0, 5)
            mixer_steps(0, STEPS * N_DIL)

            act.wait_ge(exp_done, STEPS * N_DIL)
            act.wait_ge(inv_done, STEPS * N_DIL)
            act.activation(rowsum[:, 0:96], rowsum[:, 0:96], ACT.Ln).then_inc(ln_ok, 1)
            to_natural(1, lambda dst, src: act.copy(dst, src), act)
            raw_evacuate(N_DIL + 1, 0)
            act.wait_ge(lsub_ok, 1)
            act.activation(lse_nat, lse_nat, ACT.Exp).then_inc(lexp_ok, 1)
            act.wait_ge(alpha_f, 1)
            act.copy(alpha_nat[:, :, :, 0, :], lse_nat.rearrange("p g (i h) -> p g i h", i=8)).then_inc(alpha_hi, 1)
            for g in (1, 2):
                act.wait_ge(at_done, 3)
                act.copy(alpha_st[:, g, :], PS[g][0:8, :]).then_inc(alpha_row[g], 1)
            raw_evacuate(N_DIL + 1, 1)
            act.wait_ge(comb_ok, 1)
            mixer_steps(STEPS * N_DIL, STEPS * MIX)

            act.wait_ge(pv_done, STEPS * MIX)
            act.wait_ge(ote_done, 8 * MIX)
            for k in range(6):
                src = keep[:, k * 1024:(k + 1) * 1024] if k < 4 else ob[:, (k - 4) * 1024:(k - 3) * 1024]
                act.copy(br_in[:, 0, k, :], src).then_inc(br_hi, 1)
            with act.Fori(0, N_GATE // 2) as it:
                for n in range(6):
                    m, j = divmod(n, 3)
                    c = CH0 + 3 * MIX + n
                    if j < 2:
                        act.wait_ge(w_used, it * 6 + (c + 1))
                        act.wait_ge(mixed_ok, it * 2 + m + PRIME)
                        act.activation(tmp[:, j, :], PS[j][:], ACT.Sigmoid).then_inc(sig_ok, 1)
                    act.wait_ge(w_in_s[c % 2], it * 48 + 16 * ((c + 2) // 2 + 1))
                    act.wait_ge(w_used, it * 6 + (c + 1))
                    act.copy(wsp[:, c % 2, 0, :], raw[:, c % 2, :]).then_inc(w_hi, 1)

            act.wait_ge(w_used, CH_OUT)
            for c in range(KC):
                act.wait_ge(mixed_ok, N_GATE + PRIME)
                act.copy(hspl[:, 0, c, :], kp[:, c, :]).then_inc(m_hi, 1)

            def split_hi2(n, b=None):
                loaded, count = loaded_at(n)
                if b is None:
                    act.wait_ge(loaded, 16 * count)
                    act.wait_ge(w_used, CH_OUT + max(n - 3, 0))
                else:
                    act.wait_ge(loaded, b * 32 + 16 * count)
                    act.wait_ge(w_used, b * 8 + (CH_OUT + n - 3))
                act.copy(wsp_at(n, 0), raw_at(n)).then_inc(w_hi, 1)

            split_hi2(2)
            for n in range(KC):
                split_hi2(n + 3)
                act.wait_ge(xct_done, n + 1)
                if n == 0:
                    act.wait_ge(m_lo, KC)
                act.copy(kp[:, n, :], PS[2 + n % 2][:]).then_inc(xres, 1)
                act.wait_ge(resid, n + 1)
                if n >= 1:
                    act.wait_ge(acc_ok, n + 1)
                act.activation(tmp[:, 1, :], kp[:, n, :], ACT.Square).then_inc(sq_ok, 1)
            act.wait_ge(mean_done, 1)
            act.wait_ge(acc_ok, KC + 1)
            act.activation(tmp[:, 1, :], PS[0][:], ACT.Sqrt, bias=eps_c[:]).then_inc(mean_out, 1)
            act.wait_ge(w_used, CH_OUT + KC)
            for c in range(KC):
                act.activation(hspl[:, 0, c, :], kp[:, c, :], ACT.Copy, scale=gm_g[:, c:c + 1]).then_inc(h_hi, 1)

            def mlp_block(b, last):
                for j in range(4):
                    split_hi2(KC + j + 3, b)
                    act.wait_ge(u_r, b * 4 + (j + 1) + PRIME)
                    act.wait_ge(u_lo, b * 4 + j + PRIME)
                    act.wait_ge(rstd_ok, 1)
                    act.activation(tmp[:, 1, :], tmp[:, 0, :], ACT.Square).then_inc(u_sq, 1)
                    act.wait_ge(u_sq, b * 4 + (j + 1) + PRIME)
                    act.wait_ge(w_used, b * 8 + (CH_OUT + KC))
                    act.copy(hid[:, 0, j, :], tmp[:, 1, :]).then_inc(u_hi, 1)
                for j in range(4, 8):
                    if not last or j + 3 < 8:
                        split_hi2(KC + j + 3, b)
                    if last:
                        if j == 4:
                            act.wait_ge(u_sq, FF_BLOCKS * 4 + PRIME)
                        for m in (2 * j - 8, 2 * j - 7):
                            act.wait_ge(dn_add, b * 8 + (m + 1) + PRIME)
                            if m >= 1:
                                act.wait_ge(facc, m)
                            act.activation(tmp[:, 0, :], kp[:, m, :], ACT.Square).then_inc(fsq, 1)

            with act.Fori(0, FF_BLOCKS - 1) as b:
                mlp_block(b, False)
            mlp_block(FF_BLOCKS - 1, True)
            act.wait_ge(fmean_out, 1)
            act.activation(xstat[:], xstat[:], ACT.Sqrt).then_inc(froot, 1)

        @block.vector
        def _(dve):
            for primed in (gmul, mixed_ok, u_r, u_lo, dn_add):
                dve.sem_inc(primed, 1)
            chain = [0]

            def link(ins):
                chain[0] += 1
                ins.then_inc(dchain, 1)
                dve.wait_ge(dchain, chain[0])

            def split_lo(c, half=None):
                cols = slice(0, 1024) if half is None else slice(half * HALF, (half + 1) * HALF)
                dve.wait_ge(w_hi, c + 1)
                ins = dve.tensor_tensor(wsp[:, c % 2, 1, cols], raw[:, c % 2, cols],
                                        wsp[:, c % 2, 0, cols].bitcast(F32), ALU.subtract)
                if half != 0:
                    ins.then_inc(w_lo, 1)

            for half in range(2):
                h4 = slice(4 * half, 4 * half + 4)
                dve.wait_ge(x_sq, 4 * half + 4)
                dve.tensor_scalar(xstat[:, h4], xstat[:, h4], 1.0 / D, EPS, ALU.mult, ALU.add).then_inc(x_st, 1)
                dve.wait_ge(x_root, half + 1)
                dve.reciprocal(xrstd[:, h4], xstat[:, h4]).then_inc(x_rs, 1)
                dve.wait_ge(x_rs, half + 1)
                for i in range(4):
                    t = 4 * half + i
                    dve.tensor_scalar(tmp[:, i, :], tmp[:, i, :], xrstd[:, t:t + 1], None, ALU.mult).then_inc(x_scaled, 1)
                if half == 0:
                    split_lo(0)
                else:
                    split_lo(1)
                for c in range(KC):
                    n = half * KC + c
                    dve.wait_ge(xhi, n + 1)
                    bank = PS[(n % 4) // 2][:, (n % 2) * HALF:(n % 2 + 1) * HALF]
                    cols = slice(half * HALF, (half + 1) * HALF)
                    dve.scalar_tensor_tensor(out=hspl[:, 1, c, cols], in0=bank, scalar=ga_g[:, c:c + 1],
                                             in1=hspl[:, 0, c, cols].bitcast(F32), op0=ALU.mult,
                                             op1=ALU.subtract).then_inc(xlo, 1)
            H8 = FOX_HEADS
            fz, fe, fc, fo = (tmp[0:H8, i, :] for i in range(4))
            mid = tmp[0:H8, 1, 0:512].bitcast(BF16)
            dve.wait_ge(w_used, 1)
            dve.wait_ge(xt_done, 16)
            dve.wait_ge(small_in, 48)
            dve.tensor_scalar(fz, PS[0][0:H8, :], bfor[0:H8, :], None, ALU.add).then_inc(fz_ok, 1)
            link(dve.memset(fo, 1.0))
            dve.wait_ge(fln_ok, 1)
            dve.wait_ge(fz_ok, 1)
            link(dve.scalar_tensor_tensor(out=fz, in0=fz, scalar=0.0, in1=fe, op0=ALU.min, op1=ALU.subtract))
            link(dve.tensor_tensor_scan(fc, fo, fz, 0.0, ALU.mult, ALU.add))
            dve.wait_ge(consts, N_CONST)
            link(dve.tensor_scalar(fbias[0:H8, :], fc, -1.0, None, ALU.mult))
            link(dve.scalar_tensor_tensor(out=fz, in0=fc, scalar=-1.0, in1=fbias[0:H8, :], op0=ALU.mult,
                                          op1=ALU.subtract))
            link(dve.tensor_copy(mid, fz))
            dve.tensor_copy(fbias[32:32 + H8, :], fz)
            link(dve.tensor_tensor(fz, fz, mid, ALU.subtract))
            dve.tensor_copy(fbias[64:64 + H8, :], fz).then_inc(fbias_ok, 1)
            split_lo(2)
            dve.wait_ge(fbias_ok, 1)

            def rotate(u, which, half, n):
                cols = slice(half * HALF, (half + 1) * HALF)
                x = (k_raw, q_raw(u))[which][:, cols]
                other = v_raw[:, cols]
                if n == 0:
                    dve.wait_ge(raw_out, 6 * u + 2 * which + half + 1)
                    dve.wait_ge(rope_in, 16)
                    after(dve, vt_done, 2 * u)
                    swap = list(range(8, 16)) + list(range(8)) + list(range(16, 32))
                    ins = dve.stream_shuffle(other, x, swap)
                else:
                    dve.wait_ge(roped, 16 * u + 8 * which + 4 * half + n)
                    if n == 1:
                        ins = dve.tensor_tensor(x, x, rope_c[:, cols], ALU.mult)
                    elif n == 2:
                        ins = dve.tensor_tensor(other, other, rope_s[:, cols], ALU.mult)
                    else:
                        ins = dve.tensor_tensor(x, x, other, ALU.add)
                ins.then_inc(roped, 1)

            def k_stack(u, h):
                row = 64 * h
                dve.wait_ge(k_hi, 2 * u + h + 1)
                dve.tensor_tensor(ordered(k_st[u % 2][h][64 - row:P - row], u), natural(k_raw[row:row + 64], u),
                                  ordered(k_st[u % 2][h][row:row + 64].bitcast(F32), u), ALU.subtract).then_inc(k_lo, 1)

            def q_tile(G):
                t, s = divmod(G, STEPS)
                row = 64 * (s % 2)
                dve.wait_ge(q_hi, 2 * G + 2)
                for dst in (0, 64):
                    dve.scalar_tensor_tensor(out=tile_view(q_st[dst:dst + 64, G % 3, 1, :], t),
                                             in0=tile_tokens(q_raw(t)[row:row + 64], t, s // 2), scalar=QSCALE,
                                             in1=tile_view(q_st[row:row + 64, G % 3, 0, :].bitcast(F32), t),
                                             op0=ALU.mult, op1=ALU.subtract).then_inc(q_lo, 1)

            def values_lo(t):
                for bank in range(2):
                    dve.wait_ge(v_hi, 2 * t + bank + 1)
                    dve.tensor_tensor(v_nat[:, 4 * bank:4 * bank + 4, :, 1, :],
                                      PS[2][:, bank * HALF:(bank + 1) * HALF].rearrange("p (t h d) -> p t h d", t=4, h=2),
                                      v_nat[:, 4 * bank:4 * bank + 4, :, 0, :].bitcast(F32),
                                      ALU.subtract).then_inc(v_lo, 1)

            def maxes(G):
                n = len(tiles_of(G))
                c = column(G)
                dve.wait_ge(qk_done, G + 1)
                dve.tensor_reduce(negmax[:, c:c + 1], psc[G % 2][:, 0:n * P], AX_X, ALU.max,
                                  negate=True).then_inc(max_done, 1)

            def probs_lo(G):
                for n, (a, b) in enumerate(units_of(G)):
                    u = units_before(G) + n
                    dve.wait_ge(pt_hi, u + 1)
                    dve.tensor_tensor(pt[:, G % 2, 1, a * P:b * P],
                                      PS[2][:, (u % 2) * HALF:(u % 2) * HALF + (b - a) * P],
                                      pt[:, G % 2, 0, a * P:b * P].bitcast(F32), ALU.subtract).then_inc(pt_lo, 1)

            def inverses(G):
                c = column(G)
                dve.wait_ge(exp_done, G + 1)
                dve.reciprocal(rowinv[:, c:c + 1], rowsum[:, c:c + 1]).then_inc(inv_done, 1)

            def outs(G):
                i, h = divmod(G, 2)
                c = column(G)
                dve.wait_ge(op_done, G + 1)
                dve.wait_ge(inv_done, G + 1)
                after(dve, ot_done, i - 1)
                dve.scalar_tensor_tensor(out=o_nat[:, i % 2, h * HD:(h + 1) * HD],
                                         in0=pso[:, h * P:h * P + HD], scalar=rowinv[:, c:c + 1],
                                         in1=o_part[:, h, :], op0=ALU.mult, op1=ALU.add).then_inc(on_done, 1)

            def side_work(G):
                t, s = divmod(G, STEPS)
                u = t + 1
                jobs = []
                for s0, s1, c in ((1, 1, 3 * t + 4) if t == N_DIL else (3, 4, 3 * t + 4), (8, 8, 3 * t + 5),
                                  (14, 14, 3 * t + 6)):
                    if u < MIX or c == 3 * t + 4:
                        jobs += [lambda c=c: split_lo(CH0 + c, 0)] if s == s0 else []
                        jobs += [lambda c=c: split_lo(CH0 + c, 1)] if s == s1 else []
                if u < MIX and s in (9, 15):
                    jobs.append(lambda: k_stack(u, (s - 9) // 6))
                if u < N_DIL:
                    jobs += [lambda n=n: rotate(u, n // 8, n // 4 % 2, n % 4) for n in ROTATE_OPS.get(s, ())]
                return jobs

            def mixer_steps(first, last):
                for G in range(first, last + 3):
                    t, s = divmod(G, STEPS)
                    if first <= G - 3 < last:
                        outs(G - 3)
                    jobs = side_work(G) if G < last else []
                    if G < last:
                        maxes(G)
                    for job in jobs[:1]:
                        job()
                    if first <= G - 1 < last:
                        probs_lo(G - 1)
                        inverses(G - 1)
                    if G < last and G + 2 < STEPS * MIX:
                        q_tile(G + 2)
                    if s == 1 and G < last:
                        values_lo(t)
                    for job in jobs[1:]:
                        job()

            for n in range(8):
                rotate(0, 0, n // 4, n % 4)
            split_lo(3)
            k_stack(0, 0)
            k_stack(0, 1)
            for n in range(8):
                rotate(0, 1, n // 4, n % 4)
            split_lo(4)
            q_tile(0)
            q_tile(1)
            mixer_steps(0, STEPS * N_DIL)

            dve.wait_ge(ln_ok, 1)
            dve.tensor_tensor(rowsum[:, 0:96], rowsum[:, 0:96], negmax[:, 0:96], ALU.subtract).then_inc(lse_ok, 1)
            for g in (0, 2):
                to_natural(g, lambda dst, src: dve.tensor_copy(dst, src), dve)
            dve.wait_ge(ln_done, 1)
            link(dve.tensor_copy(lse_nat, pso[:, 0:96].rearrange("p (g c) -> p g c", g=3)))
            link(dve.tensor_tensor(top, lse_nat[:, 0, :], lse_nat[:, 1, :], ALU.max))
            link(dve.tensor_tensor(top, top, lse_nat[:, 2, :], ALU.max))
            for g in range(3):
                ins = dve.tensor_tensor(lse_nat[:, g, :], lse_nat[:, g, :], top, ALU.subtract)
            ins.then_inc(lsub_ok, 1)
            dve.wait_ge(lexp_ok, 1)
            link(dve.tensor_tensor(top, lse_nat[:, 0, :], lse_nat[:, 1, :], ALU.add))
            link(dve.tensor_tensor(top, top, lse_nat[:, 2, :], ALU.add))
            link(dve.reciprocal(top, top))
            for g in range(3):
                ins = dve.tensor_tensor(lse_nat[:, g, :], lse_nat[:, g, :], top, ALU.mult)
            ins.then_inc(alpha_f, 1)
            dve.wait_ge(alpha_f, 1)
            dve.wait_ge(alpha_hi, 1)
            dve.tensor_tensor(alpha_nat[:, :, :, 1, :], lse_nat.rearrange("p g (i h) -> p g i h", i=8),
                              alpha_nat[:, :, :, 0, :].bitcast(F32), ALU.subtract).then_inc(alpha_lo, 1)
            dve.wait_ge(at_done, 3)
            dve.tensor_copy(alpha_st[:, 0, :], PS[0][0:8, :]).then_inc(alpha_row[0], 1)
            dve.wait_ge(ote_done, 8 * N_DIL)
            for n in range(6):
                pair, g = divmod(n, 3)
                dve.wait_ge(spr_done, n + 1)
                dst = ob[:, pair * 1024:(pair + 1) * 1024]
                one = dst if g == 0 else tmp[:, 6, :]
                dve.tensor_tensor(one, PS[n % 2][:], og[:, g, pair * 1024:(pair + 1) * 1024], ALU.mult).then_inc(spr_out, 1)
                dve.wait_ge(spr_out, n + 1)
                if g > 0:
                    ins = dve.tensor_tensor(dst, dst, one, ALU.add)
                    if n < 5:
                        link(ins)
                    else:
                        ins.then_inc(comb_ok, 1)
            mixer_steps(STEPS * N_DIL, STEPS * MIX)

            for k in range(6):
                src = keep[:, k * 1024:(k + 1) * 1024] if k < 4 else ob[:, (k - 4) * 1024:(k - 3) * 1024]
                dve.wait_ge(br_hi, k + 1)
                dve.tensor_tensor(br_in[:, 1, k, :], src, br_in[:, 0, k, :].bitcast(F32), ALU.subtract).then_inc(br_lo, 1)
            with dve.Fori(0, N_GATE // 2) as it:
                for n in range(6):
                    m, j = divmod(n, 3)
                    c = CH0 + 3 * MIX + n
                    if j == 2:
                        dve.wait_ge(w_used, it * 6 + (c + 1))
                        for a in range(2):
                            dve.wait_ge(sig_ok, it * 4 + (2 * m + a + 1) + PRIME)
                            dve.tensor_tensor(tmp[:, a, :], tmp[:, a, :], PS[2 + a][:], ALU.mult).then_inc(gmul, 1)
                        dve.wait_ge(gmul, it * 4 + (2 * m + 2) + PRIME)
                        dve.tensor_tensor(keep[:, bass.ds(it * 2048 + m * 1024, 1024)], tmp[:, 0, :], tmp[:, 1, :],
                                          ALU.add).then_inc(mixed_ok, 1)
                    dve.wait_ge(w_hi, it * 6 + (c + 3))
                    dve.tensor_tensor(wsp[:, c % 2, 1, :], raw[:, c % 2, :], wsp[:, c % 2, 0, :].bitcast(F32),
                                      ALU.subtract).then_inc(w_lo, 1)

            dve.wait_ge(mixed_ok, N_GATE + PRIME)
            for c in range(KC):
                dve.wait_ge(m_hi, c + 1)
                dve.tensor_tensor(hspl[:, 1, c, :], kp[:, c, :], hspl[:, 0, c, :].bitcast(F32), ALU.subtract).then_inc(m_lo, 1)

            def split_lo2(n, b=0):
                dve.wait_ge(w_hi, b * 8 + (CH_OUT + n + 1))
                dve.tensor_tensor(wsp_at(n, 1), raw_at(n), wsp_at(n, 0).bitcast(F32), ALU.subtract).then_inc(w_lo, 1)

            dve.memset(tmp[:, 3, :], 0.0).then_inc(acc_ok, 1)
            split_lo2(2)
            for n in range(KC):
                split_lo2(n + 3)
                dve.wait_ge(w_used, CH_OUT + n + 1)
                dve.wait_ge(xres, n + 1)
                dve.tensor_tensor(kp[:, n, :], kp[:, n, :], PS[n % 2][:], ALU.add).then_inc(resid, 1)
                dve.wait_ge(sq_ok, n + 1)
                dve.wait_ge(acc_ok, n + 1)
                dve.tensor_tensor(tmp[:, 3, :], tmp[:, 3, :], tmp[:, 1, :], ALU.add).then_inc(acc_ok, 1)
            for c in range(KC):
                dve.wait_ge(h_hi, c + 1)
                dve.scalar_tensor_tensor(out=hspl[:, 1, c, :], in0=kp[:, c, :], scalar=gm_g[:, c:c + 1],
                                         in1=hspl[:, 0, c, :].bitcast(F32), op0=ALU.mult,
                                         op1=ALU.subtract).then_inc(h_lo, 1)
            dve.wait_ge(mean_out, 1)
            dve.reciprocal(tmp[:, 3, :], tmp[:, 1, :]).then_inc(rstd_ok, 1)
            dve.wait_ge(rstd_ok, 1)

            def mlp_block(b, last):
                for j in range(4):
                    split_lo2(KC + j + 3, b)
                    dve.wait_ge(w_used, b * 8 + (CH_OUT + KC + j + 1))
                    dve.wait_ge(u_sq, b * 4 + j + PRIME)
                    dve.scalar_tensor_tensor(out=tmp[:, 0, :], in0=PS[j % 2][:], scalar=0.0, in1=tmp[:, 3, :],
                                             op0=ALU.max, op1=ALU.mult).then_inc(u_r, 1)
                    dve.wait_ge(u_hi, b * 4 + (j + 1))
                    dve.tensor_tensor(hid[:, 1, j, :], tmp[:, 1, :], hid[:, 0, j, :].bitcast(F32),
                                      ALU.subtract).then_inc(u_lo, 1)
                if last:
                    link(dve.memset(tmp[:, 3, :], 0.0))
                for j in range(4, 8):
                    if not last or j + 3 < 8:
                        split_lo2(KC + j + 3, b)
                    for m in (2 * j - 8, 2 * j - 7):
                        if m % 2:
                            dve.wait_ge(w_used, b * 8 + (CH_OUT + KC + 4 + m // 2 + 1))
                        else:
                            dve.wait_ge(dn_even, b * 4 + (m // 2 + 1))
                        dve.tensor_tensor(kp[:, m, :], kp[:, m, :], PS[2 + m % 2][:], ALU.add).then_inc(dn_add, 1)
                        if last:
                            dve.wait_ge(fsq, m + 1)
                            if m:
                                dve.wait_ge(facc, m)
                            dve.tensor_tensor(tmp[:, 3, :], tmp[:, 3, :], tmp[:, 0, :], ALU.add).then_inc(facc, 1)

            with dve.Fori(0, FF_BLOCKS - 1) as b:
                mlp_block(b, False)
            mlp_block(FF_BLOCKS - 1, True)
            dve.wait_ge(fmean, 1)
            dve.tensor_scalar(xstat[:], PS[0][:, 0:8], EPS, None, ALU.add).then_inc(fmean_out, 1)
            dve.wait_ge(froot, 1)
            dve.reciprocal(xrstd[:], xstat[:]).then_inc(frstd, 1)
            dve.wait_ge(frstd, 1)
            dve.wait_ge(gfin_in, 16)
            for i in range(8):
                dve.wait_ge(ft_done, i + 1)
                if i >= 2:
                    dve.wait_ge(y_out[i % 2], 16 * (i // 2))
                dve.scalar_tensor_tensor(out=tmp[:, i % 2, :], in0=PS[1 + i % 3][:], scalar=xrstd[:, i:i + 1],
                                         in1=tmp[:, 2, :], op0=ALU.mult, op1=ALU.mult).then_inc(y_ok, 1)


def kernel(**inputs):
    import numpy as np
    import concourse.bacc as bacc
    from concourse.bass_utils import run_bass_kernel_spmd

    f = {k: np.asarray(v) for k, v in inputs.items()}
    half = HD // 8
    inv = np.power(np.float32(500000.0), -np.arange(half, dtype=np.float32) * np.float32(2.0) / np.float32(2 * half))
    ang = np.arange(S, dtype=np.float32)[None, :] * inv.astype(np.float32)[:, None]
    rope = np.zeros((P, 2, S), np.float32)
    rope[:, 0] = 1.0
    for h in range(2):
        for part in range(2):
            rows = slice(h * HD + part * half, h * HD + (part + 1) * half)
            rope[rows, 0] = np.cos(ang)
            rope[rows, 1] = np.sin(ang) * (1.0 if part else -1.0)
    arrays = {
        "x": np.ascontiguousarray(f["x"][0]),
        "g_attn": np.ascontiguousarray(f["norm_attn_g"][0].reshape(KC, P).T),
        "w_in": np.ascontiguousarray(f["w_in"][0]),
        "b_forget": np.ascontiguousarray(f["b_forget"][0].reshape(FOX_HEADS, 1)),
        "w_branch": np.concatenate([f["w_branch_a"][0], f["w_branch_b"][0]], axis=0),
        "w_out": np.ascontiguousarray(f["w_out"][0]),
        "g_mlp": np.ascontiguousarray(f["norm_mlp_g"][0].reshape(KC, P).T),
        "w_up": np.ascontiguousarray(f["w_up"][0]),
        "w_down": np.ascontiguousarray(f["w_down"][0]),
        "g_final": np.ascontiguousarray(np.broadcast_to(f["norm_final_g"], (P, D))),
        "rope": rope,
    }
    nc = bacc.Bacc("TRN2", target_bir_lowering=False, num_devices=1)
    args = [nc.dram_tensor(f"in_{k}", a.shape, mybir.dt.from_np(a.dtype), kind="ExternalInput").ap()
            for k, a in arrays.items()]
    out = nc.dram_tensor("out_y", (S, D), F32, kind="ExternalOutput").ap()
    build(nc, *args, out)
    r = run_bass_kernel_spmd(nc, [{f"in_{k}": a for k, a in arrays.items()}], core_ids=[0])
    return r.results[0]["out_y"].reshape(1, S, D)
```

```python
from contextlib import ExitStack

import concourse.bass as bass
from concourse import mybir

ALU = mybir.AluOpType
ACT = mybir.ActivationFunctionType
BF16 = mybir.dt.bfloat16
F32 = mybir.dt.float32
F32R = mybir.dt.float32r
AX_X = mybir.AxisListType.X

P = 128
D = 1024
S = 1024
KC = D // P
HD = 64
HALF = 512
EPS = 1e-6
NEG = -1e30
FOX_HEADS = 8
FOX_W = FOX_HEADS * HD
DILATIONS = (1, 4, 16)
DIL_W = 4 * HD * len(DILATIONS)
COL_FA = 3 * FOX_W
COL_QB = COL_FA + FOX_HEADS
COL_KB = COL_QB + DIL_W
COL_VB = COL_KB + DIL_W
COL_GA = COL_VB + DIL_W
COL_GB = COL_GA + D
QSCALE = float(HD) ** -0.5
FF_BLOCKS = 8
N_DIL = 2 * len(DILATIONS)
N_FOX = FOX_HEADS // 2
N_GATE = KC
CH0 = 1
CH_OUT = CH0 + 3 * (N_DIL + N_FOX + N_GATE)
PRIME = 1
STEPS = 16
MIX = N_DIL + N_FOX


def group_steps(t):
    if t == N_DIL:
        return (), (), (2, 3, 4, 5), (6, 7, 8, 9), (10, 11, 12), (13, 14, 15)
    if t == MIX - 1:
        return (0, 1, 2, 3), (4, 5, 6, 7), (8, 9, 10, 11), (12, 13, 14, 15)
    return (0, 1, 2), (3, 4, 5), (6, 7, 8), (9, 10, 11), (12, 13), (14, 15)


def group_out(t, s):
    return next((g for g, steps in enumerate(group_steps(t)) if s - 1 in steps[-1:]), None)


ROTATE_OPS = {3: (0,), 4: (1,), 5: (2, 3), 6: (4, 5), 7: (6, 7), 9: (8,), 10: (9,), 11: (10, 11),
              12: (12, 13), 13: (14, 15)}


def dil_of(t):
    return DILATIONS[t // 2] if t < N_DIL else None


def column(G):
    t, s = divmod(G, STEPS)
    if t >= N_DIL:
        return G
    return (((t // 2) * 8 + s // 2) * 2 + t % 2) * 2 + s % 2


def key_tiles(t, i):
    dil = dil_of(t)
    if dil is None:
        return [(j, "causal" if j == i else None) for j in range(i + 1)]
    if dil == 16:
        return [(i, "twoblock")]
    if i % (8 // dil) == 0:
        return [(i, "causal")]
    return [(i - 1, "prev"), (i, "causal")]


def tiles_of(G):
    return key_tiles(G // STEPS, G % STEPS // 2)


def units_of(G):
    n = len(tiles_of(G))
    return [(a, min(a + 4, n)) for a in range(0, n, 4)]


def units_before(G):
    return sum(len(units_of(x)) for x in range(G))


def tile_tokens(ap, t, i):
    d = dil_of(t)
    if d in (None, 1):
        return ap[:, i * P:(i + 1) * P]
    v = ap.rearrange("p (l r) -> p r l", r=d)
    if d == 4:
        return v[:, i // 2, (i % 2) * P:(i % 2 + 1) * P]
    return v[:, 2 * i:2 * i + 2, :]


def tile_view(ap, t):
    return ap.rearrange("p (r l) -> p r l", r=2) if dil_of(t) == 16 else ap


def natural(ap, t):
    d = dil_of(t)
    return ap if d in (None, 1) else ap.rearrange("p (l r) -> p r l", r=d)


def ordered(ap, t):
    d = dil_of(t)
    return ap if d in (None, 1) else ap.rearrange("p (r l) -> p r l", r=d)


def after(eng, sem, n):
    if n > 0:
        eng.wait_ge(sem, n)


def build(nc, x, g_attn, w_in, b_forget, w_branch, w_out, g_mlp, w_up, w_down, g_final, rope, out):
    w_in_v = w_in.rearrange("(k p) n -> p k n", p=P)
    w_br_v = w_branch.rearrange("(k p) n -> p k n", p=P)
    w_out_v = w_out.rearrange("(k p) n -> p k n", p=P)
    w_up_v = w_up.rearrange("(k p) n -> p k n", p=P)
    w_dn_v = w_down.rearrange("(f p) n -> p f n", p=P)
    x_t = x.rearrange("(t p) d -> p t d", p=P)
    out_t = out.rearrange("(t p) d -> p t d", p=P)

    with ExitStack() as ctx:
        def sb(name, shape, dt):
            return ctx.enter_context(nc.sbuf_tensor(name, shape, dt))

        def sem(name):
            return ctx.enter_context(nc.semaphore(name))

        hspl = sb("hspl", [P, 2, KC, S], F32R)
        work = sb("work", [P, 12 * 1024], F32R)
        keep = sb("keep", [P, 8 * 1024], F32)
        raw = sb("raw", [P, 2, 1024], F32)
        wsp = sb("wsp", [P, 2, 2, 1024], F32R)
        tmp = sb("tmp", [P, 7, 1024], F32)
        fbias = sb("fbias", [P, S], BF16)
        fsel = sb("fsel", [P, FOX_HEADS, P], BF16)
        ident = sb("ident", [P, P], F32)
        ident_b = sb("ident_b", [P, P], BF16)
        masks = sb("masks", [P, 3, P], BF16)
        mean_w = sb("mean_w", [P, P], F32)
        spread_f = sb("spread_f", [P, 2, P], F32)
        spread = sb("spread", [P, 2, P], F32R)
        o_nat = sb("o_nat", [P, 2, P], F32)
        o_part = sb("o_part", [P, 2, HD], F32)
        negmax = sb("negmax", [P, STEPS * MIX], F32)
        rowsum = sb("rowsum", [P, STEPS * MIX], F32)
        rowinv = sb("rowinv", [P, STEPS * MIX], F32)
        xstat = sb("xstat", [P, KC], F32)
        xrstd = sb("xrstd", [P, KC], F32)
        ga_g = sb("ga_g", [P, KC], F32)
        gm_g = sb("gm_g", [P, KC], F32)
        eps_c = sb("eps_c", [P, 1], F32)
        bfor = sb("bfor", [P, 1], F32)
        PS = [ctx.enter_context(nc.psum_tensor(f"ps{i}", [P, 1024], F32)) for i in range(4)]
        MASK = {"causal": masks[:, 0, :], "prev": masks[:, 1, :], "twoblock": masks[:, 2, :]}

        k_st = [[work[:, (2 * b + h) * 1024:(2 * b + h + 1) * 1024] for h in range(2)] for b in range(2)]
        v_nat = work[:, 4 * 1024:6 * 1024].rearrange("p (t h s d) -> p t h s d", t=8, h=2, s=2)
        q_st = work[:, 6144:6912].rearrange("p (b s c) -> p b s c", b=3, s=2)
        pt = work[:, 8 * 1024:12 * 1024].rearrange("p (b s c) -> p b s c", b=2, s=2)
        alpha_nat = work[:, 11264:11456].rearrange("p (g i s h) -> p g i s h", g=3, i=8, s=2)
        alpha_st = work[0:8, 8192:8192 + 3072].rearrange("p (g c) -> p g c", g=3)
        k_raw, v_raw = tmp[:, 4, :], tmp[:, 5, :]
        rope_c, rope_s = tmp[:, 0, :], tmp[:, 1, :]
        psc = [PS[0], PS[1]]

        def psp(u, g):
            return (PS[0] if u <= N_DIL and g % 2 else PS[3])[:, HALF:2 * HALF]

        pso = PS[3][:, 0:HALF]
        lse_nat = tmp[:, 6, 0:96].rearrange("p (g c) -> p g c", g=3)
        top = tmp[:, 6, 96:128]
        lrow = [tmp[0:4, 0, :], tmp[0:4, 1, :], tmp[0:4, 3, :]]

        def q_raw(t):
            return tmp[:, 2 + t % 2, :]

        def probs(G):
            if G < STEPS * N_DIL:
                return tmp[:, 6, (G % 2) * 256:(G % 2 + 1) * 256]
            return tmp[:, G % 2, :]

        br_in = work[:, :].rearrange("p (s k c) -> p s k c", s=2, k=6)
        h_low = work[:, 0:8192].rearrange("p (s k c) -> p s k c", s=2, k=4)
        hid = hspl[:, :, 0:4, :]

        def mlp_in(part, k):
            return h_low[:, part, k, :] if k < 4 else hspl[:, part, k, :]

        og = keep[:, 0:6144].rearrange("p (g c) -> p g c", g=3)
        ob = keep[:, 6144:8192]
        kp = keep[:, :].rearrange("p (k c) -> p k c", k=KC)

        y_tile = [tmp[:, 5, :], tmp[:, 6, :], tmp[:, 4, :], raw[:, 0, :], raw[:, 1, :], tmp[:, 0, :], tmp[:, 1, :],
                  tmp[:, 3, :]]
        gate0 = (tmp[:, 4, :], tmp[:, 2, :])

        def x_tile(i):
            return keep[:, i * 1024:(i + 1) * 1024]

        forget = [x_tile(i)[0:FOX_HEADS] for i in range(4, 8)]

        def raw_at(n):
            return (raw[:, 1, :], raw[:, 0, :], tmp[:, 2, :], tmp[:, 4, :])[n % 4]

        def wsp_at(n, part):
            return (wsp[:, 1, part, :], wsp[:, 0, part, :], work[:, 8192 + part * 1024:9216 + part * 1024],
                    work[:, 10240 + part * 1024:11264 + part * 1024])[n % 4]

        def loaded_at(n):
            return ((w_in_s[1], 28 + n // 4), (w_in_s[0], 29 + n // 4), (w_in_s[2], 1 + n // 4),
                    (w_in_s[3], 1 + n // 4))[n % 4]

        def to_natural(g, copy, eng):
            eng.wait_ge(lt_done, g + 1)
            dst, src, dil = lrow[g], PS[g][0:4, :], DILATIONS[g]
            if dil > 1:
                dst = dst.rearrange("p (l r) -> p r l", r=dil)
                src = src.rearrange("p (r l) -> p r l", r=dil)
            copy(dst, src).then_inc(lt_out[g], 1)

        x_in = [sem(f"x_in{i}") for i in range(8)]
        small_in = sem("small_in")
        rope_in = sem("rope_in")
        xcol_in = [sem(f"xcol_in{i}") for i in range(2)]
        gfin_in = sem("gfin_in")
        w_in_s = [sem(f"w_loaded{i}") for i in range(4)]
        w_hi = sem("w_hi")
        w_lo = sem("w_lo")
        w_used = sem("w_used")
        consts = sem("consts")
        spread_ok = sem("spread_ok")
        x_sq = sem("x_sq")
        x_st = sem("x_st")
        x_root = sem("x_root")
        x_rs = sem("x_rs")
        x_scaled = sem("x_scaled")
        xt_done = sem("xt_done")
        xhi = sem("xhi")
        xlo = sem("xlo")
        dchain = sem("dchain")
        achain = sem("achain")
        fz_ok = sem("fz_ok")
        fln_ok = sem("fln_ok")
        fbias_ok = sem("fbias_ok")
        raw_out = sem("raw_out")
        roped = sem("roped")
        half_done = sem("half_done")
        k_hi = sem("k_hi")
        k_lo = sem("k_lo")
        q_hi = sem("q_hi")
        q_lo = sem("q_lo")
        vt_done = sem("vt_done")
        v_hi = sem("v_hi")
        v_lo = sem("v_lo")
        qk_done = sem("qk_done")
        max_done = sem("max_done")
        exp_done = sem("exp_done")
        inv_done = sem("inv_done")
        tr_done = sem("tr_done")
        pt_hi = sem("pt_hi")
        pt_lo = sem("pt_lo")
        pv_done = sem("pv_done")
        op_done = sem("op_done")
        on_done = sem("on_done")
        ot_done = sem("ot_done")
        ote_done = sem("ote_done")
        ln_ok = sem("ln_ok")
        lse_ok = sem("lse_ok")
        lt_done = sem("lt_done")
        lt_out = [sem(f"lt_out{g}") for g in range(3)]
        ln_done = sem("ln_done")
        lsub_ok = sem("lsub_ok")
        lexp_ok = sem("lexp_ok")
        alpha_f = sem("alpha_f")
        alpha_hi = sem("alpha_hi")
        alpha_lo = sem("alpha_lo")
        at_done = sem("at_done")
        alpha_row = [sem(f"alpha_row{g}") for g in range(3)]
        spr_done = sem("spr_done")
        spr_out = sem("spr_out")
        comb_ok = sem("comb_ok")
        br_hi = sem("br_hi")
        br_lo = sem("br_lo")
        sig_ok = sem("sig_ok")
        gmul = sem("gmul")
        mixed_ok = sem("mixed_ok")
        m_hi = sem("m_hi")
        m_lo = sem("m_lo")
        xct_done = sem("xct_done")
        xres = sem("xres")
        resid = sem("resid")
        sq_ok = sem("sq_ok")
        acc_ok = sem("acc_ok")
        mean_done = sem("mean_done")
        mean_out = sem("mean_out")
        rstd_ok = sem("rstd_ok")
        h_hi = sem("h_hi")
        h_lo = sem("h_lo")
        u_r = sem("u_r")
        u_sq = sem("u_sq")
        u_hi = sem("u_hi")
        u_lo = sem("u_lo")
        dn_even = sem("dn_even")
        dn_add = sem("dn_add")
        fsq = sem("fsq")
        facc = sem("facc")
        fmean = sem("fmean")
        fmean_out = sem("fmean_out")
        froot = sem("froot")
        frstd = sem("frstd")
        ft_done = sem("ft_done")
        y_ok = sem("y_ok")
        y_out = sem("y_out")

        block = ctx.enter_context(nc.Block())

        @block.sync
        def _(sp):
            def load_chunk(slot, src, dst=None):
                dst = raw[:, slot, :] if dst is None else dst
                n = src.shape[1] * src.shape[2]
                sp.dma_start(dst[:, 0:n].rearrange("p (k c) -> p k c", k=src.shape[1]), src).then_inc(w_in_s[slot], 16)

            for i in range(4):
                sp.dma_start(x_tile(i), x_t[:, i, :]).then_inc(x_in[i], 16)
            sp.dma_start(ga_g[:], g_attn).then_inc(small_in, 16)
            sp.dma_start(gm_g[:], g_mlp).then_inc(small_in, 16)
            sp.dma_start(bfor[0:FOX_HEADS, :], b_forget).then_inc(small_in, 16)
            load_chunk(0, w_in_v[:, :, COL_FA:COL_FA + P])
            for i in range(4, 8):
                sp.dma_start(x_tile(i), x_t[:, i, :]).then_inc(x_in[i], 16)
            load_chunk(1, w_in_v[:, :, COL_KB:COL_KB + P])
            sp.dma_start(tmp[:, 0:2, :], rope).then_inc(rope_in, 16)
            for c in range(2, CH_OUT):
                t, j = divmod(c - CH0, 3)
                t, j = {2: (MIX + 1, 0), 3: (MIX, 2), 4: (MIX + 1, 1)}.get(c - CH0 - 3 * MIX, (t, j))
                m = (t if t < N_DIL else t - N_DIL if t < MIX else t - MIX) * P
                cols = ((COL_KB, COL_QB, COL_VB) if t < N_DIL else (FOX_W, 0, 2 * FOX_W) if t < MIX
                        else (COL_GA, COL_GB, 0))
                src = w_br_v[:, :, m:m + P] if t >= MIX and j == 2 else w_in_v[:, :, cols[j] + m:cols[j] + m + P]
                sp.wait_ge(w_lo, c - 1)
                load_chunk(c % 2, src)

            def xcol(m):
                sp.dma_start(tmp[:, 5 + m % 2, :].rearrange("p (t c) -> p t c", t=8),
                             x_t[:, :, m * P:m * P + P]).then_inc(xcol_in[m % 2], 16)

            SLOT = (1, 0, 2, 3)
            sp.wait_ge(vt_done, 2 * MIX)
            sp.wait_ge(exp_done, STEPS * MIX)
            xcol(0)
            xcol(1)
            for n in range(4):
                sp.wait_ge(w_lo, CH_OUT - 1 + min(n, 1))
                load_chunk(SLOT[n], w_out_v[:, :, n * P:(n + 1) * P], raw_at(n))
            for n in range(KC):
                if n + 2 < KC:
                    sp.wait_ge(xct_done, n + 1)
                    xcol(n + 2)
                if n + 4 < KC:
                    sp.wait_ge(w_lo, CH_OUT + n + 1)
                    load_chunk(SLOT[n % 4], w_out_v[:, :, (n + 4) * P:(n + 5) * P], raw_at(n + 4))
            with sp.Fori(0, FF_BLOCKS) as b:
                for c in range(8):
                    sp.wait_ge(w_lo, b * 8 + (CH_OUT + KC + c - 4 + 1))
                    if c < 4:
                        src = w_up_v[:, :, bass.ds(b * 512 + c * P, P)]
                    else:
                        src = w_dn_v[:, bass.ds(b * 4, 4), (c - 4) * 256:(c - 3) * 256]
                    load_chunk(SLOT[c % 4], src, raw_at(c))
            sp.wait_ge(w_lo, CH_OUT + KC + 8 * FF_BLOCKS)
            sp.dma_start(tmp[:, 2, :], g_final).then_inc(gfin_in, 16)
            for i in range(8):
                sp.wait_ge(y_ok, i + 1)
                sp.dma_start(out_t[:, i, :], y_tile[i]).then_inc(y_out, 16)
            sp.wait_ge(y_out, 16 * 8)

        @block.gpsimd
        def _(pool):
            n = [0]

            def step(ins):
                n[0] += 1
                ins.then_inc(consts, 1)

            def settle():
                pool.wait_ge(consts, n[0])

            step(pool.memset(ident[:], 0.0))
            step(pool.memset(ident_b[:], 0.0))
            step(pool.memset(masks[:], 0.0))
            step(pool.memset(mean_w[:], 1.0 / D))
            step(pool.memset(eps_c[:], EPS))
            step(pool.memset(fbias[:], 0.0))
            step(pool.memset(fsel[:], 0.0))
            step(pool.memset(spread_f[:], 0.0))
            settle()
            for m in (ident, ident_b):
                step(pool.affine_select(out=m[:], in_=m[:], compare_op=ALU.not_equal, fill=1.0, base=0,
                                        pattern=[[-1, P]], channel_multiplier=1))
            step(pool.affine_select(out=masks[:, 0, :], in_=masks[:, 0, :], compare_op=ALU.is_ge, fill=NEG,
                                    base=0, pattern=[[-1, P]], channel_multiplier=1))
            step(pool.affine_select(out=masks[:, 1, :], in_=masks[:, 1, :], compare_op=ALU.is_ge, fill=NEG,
                                    base=0, pattern=[[1, P]], channel_multiplier=-1))
            step(pool.affine_select(out=masks[:, 2, :], in_=masks[:, 2, :], compare_op=ALU.is_ge, fill=NEG,
                                    base=0, pattern=[[-1, P]], channel_multiplier=1))
            settle()
            step(pool.affine_select(out=masks[:, 2, 0:64], in_=masks[:, 2, 0:64], compare_op=ALU.is_ge, fill=NEG,
                                    base=63, pattern=[[0, 64]], channel_multiplier=-1))
            for r in range(3):
                settle()
                step(pool.affine_select(out=fsel[:], in_=fsel[:], compare_op=ALU.not_equal, fill=1.0, base=-32 * r,
                                        pattern=[[-1, FOX_HEADS], [0, P]], channel_multiplier=1))
            sv = spread_f[:].rearrange("p a (h d) -> p a h d", h=2)
            for r in range(2):
                settle()
                step(pool.affine_select(out=sv, in_=sv, compare_op=ALU.not_equal, fill=1.0, base=-4 * r,
                                        pattern=[[-2, 2], [-1, 2], [0, HD]], channel_multiplier=1))

        N_CONST = 8 + 5 + 1 + 3 + 2

        @block.tensor
        def _(pe):
            def products_by_chunk(ps, w, mv, ready, n0):
                for k in range(KC):
                    pe.wait_ge(ready, n0 + k + 1)
                    for half in range(2):
                        cols = slice(half * HALF, (half + 1) * HALF)
                        for n, (wp, mp) in enumerate(((0, 0), (0, 1), (1, 0))):
                            ins = pe.matmul(ps[:, cols], w(wp, k), mv(mp, k)[:, cols], start=(k == 0 and n == 0),
                                            stop=(k == KC - 1 and n == 2), skip_group_check=True)
                return ins

            def split_products(ps, w, mv, ks):
                ins = None
                for half in range(2):
                    cols = slice(half * HALF, (half + 1) * HALF)
                    for k in range(ks):
                        for n, (wp, mp) in enumerate(((0, 0), (0, 1), (1, 0))):
                            ins = pe.matmul(ps[:, cols], w(wp, k), mv(mp, k)[:, cols],
                                            start=(k == 0 and n == 0), stop=(k == ks - 1 and n == 2))
                return ins

            def w_of(c):
                return lambda part, k: wsp[:, c % 2, part, k * P:(k + 1) * P]

            def h_at(part, k):
                return hspl[:, part, k, :]

            pe.wait_ge(consts, N_CONST)
            for half in range(2):
                for c in range(KC):
                    n = half * KC + c
                    if c == 0:
                        pe.wait_ge(x_scaled, 4 * half + 4)
                    if n >= 4:
                        pe.wait_ge(xlo, n - 3)
                    bank = PS[(n % 4) // 2][:, (n % 2) * HALF:(n % 2 + 1) * HALF]
                    for t in range(4):
                        ins = pe.transpose(bank[:, t * P:(t + 1) * P], x_tile(4 * half + t)[:, c * P:(c + 1) * P], ident[:])
                    ins.then_inc(xt_done, 1)
                cols = slice(half * HALF, (half + 1) * HALF)
                if half == 0:
                    pe.wait_ge(w_lo, 1)
                for k in range(KC):
                    pe.wait_ge(xlo, 8 * half + k + 1)
                    for n, (wp, mp) in enumerate(((0, 0), (0, 1), (1, 0))):
                        ins = pe.matmul(PS[2][:, cols], w_of(0)(wp, k), hspl[:, mp, k, cols],
                                        start=(k == 0 and n == 0), stop=(k == KC - 1 and n == 2))
            ins.then_inc(w_used, 1)

            def project(u, g, a, b):
                c = CH0 + 3 * u + g // 2
                cols = slice((g % 2) * HALF, (g % 2 + 1) * HALF)
                if a == 0:
                    after(pe, raw_out, 6 * u + g - (1 if u <= N_DIL and g else 0))
                    pe.wait_ge(w_lo, c + 1)
                for n in range(a, b):
                    k, (wp, mp) = n // 3, ((0, 0), (0, 1), (1, 0))[n % 3]
                    ins = pe.matmul(psp(u, g), wsp[:, c % 2, wp, k * P:(k + 1) * P], hspl[:, mp, k, cols],
                                    start=(n == 0), stop=(n == 23), skip_group_check=True)
                if b == 24:
                    ins.then_inc(w_used if g % 2 else half_done, 1)

            def project_part(G, part):
                t, s = divmod(G, STEPS)
                if t < MIX:
                    for g, steps in enumerate(group_steps(t)):
                        if s in steps:
                            per = 24 // len(steps)
                            a = (s - steps[0]) * per
                            project(t + 1, g, a + per * part // 3, a + per * (part + 1) // 3)

            def scores(G):
                t, s = divmod(G, STEPS)
                h = s % 2
                tiles = tiles_of(G)
                if s < 2:
                    pe.wait_ge(k_lo, 2 * t + s + 1)
                if G == STEPS * N_DIL + 1:
                    pe.wait_ge(spr_out, 6)
                pe.wait_ge(q_lo, 2 * G + 2)
                after(pe, exp_done, G - 1)
                ps = psc[G % 2]
                base = tiles[0][0]
                end = tiles[-1][0] + 1 - base
                for c0 in range(0, end, 4):
                    n = min(4, end - c0)
                    o = ps[:, c0 * P:(c0 + n) * P]
                    kc = slice((base + c0) * P, (base + c0 + n) * P)
                    ops = [(q_st[:, G % 3, 0, :], k_st[t % 2][h][:, kc], o),
                           (q_st[:, G % 3, 1, :], k_st[t % 2][h][:, kc], o)]
                    if t >= N_DIL:
                        ops.append((fsel[:, 2 * (t - N_DIL) + h, :], fbias[:, kc], o))
                    for j, mask in tiles:
                        if mask and c0 <= j - base < c0 + n:
                            a = (j - base) * P
                            ops.append((ident_b[:], MASK[mask], ps[:, a:a + P]))
                    for m, (lt, rh, oo) in enumerate(ops):
                        ins = pe.matmul(oo, lt, rh, start=(m == 0), stop=(m == len(ops) - 1), skip_group_check=True)
                ins.then_inc(qk_done, 1)

            def transposes(G):
                pe.wait_ge(exp_done, G + 1)
                if G % STEPS == 1:
                    pe.wait_ge(v_lo, 2 * (G // STEPS) + 2)
                for n, (a, b) in enumerate(units_of(G)):
                    u = units_before(G) + n
                    after(pe, pt_lo, u - 1)
                    for k in range(a, b):
                        ins = pe.transpose(PS[2][:, (u % 2) * HALF + (k - a) * P:(u % 2) * HALF + (k - a + 1) * P],
                                           probs(G)[:, k * P:(k + 1) * P], ident[:])
                    ins.then_inc(tr_done, 1)

            def out_transpose(i):
                pe.wait_ge(on_done, 2 * i + 2)
                pe.transpose(pso[:, 256:256 + P], o_nat[:, i % 2, :], ident[:]).then_inc(ot_done, 1)

            def values(G):
                t, s = divmod(G, STEPS)
                tiles = tiles_of(G)
                pe.wait_ge(pt_lo, units_before(G + 1))
                pe.wait_ge(v_lo, 2 * t + 2)
                after(pe, on_done, G)
                after(pe, ote_done, (G - 1) // 2)
                o = pso[:, (s % 2) * P:(s % 2 + 1) * P]
                for part in range(2):
                    for n, (j, _) in enumerate(tiles):
                        ins = pe.matmul(o, pt[:, G % 2, part, n * P:(n + 1) * P],
                                        v_nat[:, j, s % 2, :, :].rearrange("p s d -> p (s d)"),
                                        start=(part == 0 and n == 0), stop=(part == 1 and n == len(tiles) - 1))
                ins.then_inc(pv_done, 1)

            def value_transposes(t):
                pe.wait_ge(raw_out, 6 * t + 6)
                pe.wait_ge(pt_lo, units_before(STEPS * t + 1))
                for i in range(8):
                    ins = pe.transpose(PS[2][:, i * P:(i + 1) * P], v_raw[:, i * P:(i + 1) * P], ident[:])
                    if i % 4 == 3:
                        ins.then_inc(vt_done, 1)

            def mixer_steps(first, last):
                for G in range(first, last + 4):
                    if G < last:
                        scores(G)
                        project_part(G, 0)
                    if first <= G - 1 < last:
                        transposes(G - 1)
                    if G < last:
                        project_part(G, 1)
                        project_part(G, 2)
                    if G % 2 == 0 and G - 4 >= first:
                        out_transpose((G - 4) // 2)
                    if first <= G - 2 < last:
                        values(G - 2)
                    if G % STEPS == 1 and G < last:
                        value_transposes(G // STEPS)

            for g in range(6):
                project(0, g, 0, 24)
            pe.wait_ge(fz_ok, 1)
            mixer_steps(0, STEPS * N_DIL)

            project(N_DIL + 1, 0, 0, 8)
            pe.wait_ge(lse_ok, 1)
            pe.wait_ge(exp_done, STEPS * N_DIL)
            pe.wait_ge(pt_lo, STEPS * N_DIL)
            lse_v = rowsum[:, 0:96].rearrange("p (g i c) -> p g i c", g=3, i=8)
            for g in range(3):
                for i in range(8):
                    ins = pe.transpose(PS[g][0:4, i * P:(i + 1) * P], lse_v[:, g, i, :], ident[:])
                ins.then_inc(lt_done, 1)
            project(N_DIL + 1, 0, 8, 16)
            pe.wait_ge(ote_done, 8 * N_DIL)
            for g in range(3):
                pe.wait_ge(lt_out[g], 1)
                for i in range(8):
                    ins = pe.transpose(pso[:, g * 32 + i * 4:g * 32 + i * 4 + 4], lrow[g][:, i * P:(i + 1) * P],
                                       ident[0:4, 0:4])
            ins.then_inc(ln_done, 1)
            project(N_DIL + 1, 0, 16, 24)
            pe.wait_ge(alpha_lo, 1)
            for g in range(3):
                for i in range(8):
                    ins = pe.transpose(PS[g][0:8, i * P:(i + 1) * P],
                                       alpha_nat[:, g, i, :, :].rearrange("p s h -> p (s h)").bitcast(F32), ident[:])
                ins.then_inc(at_done, 1)
            pe.wait_ge(spread_ok, 1)
            for n in range(6):
                g, pair = divmod(n, 2)
                project(N_DIL + 1, 1, 4 * n, 4 * n + 4)
                pe.wait_ge(alpha_row[g], 1)
                if n == 1:
                    pe.wait_ge(alpha_row[1], 1)
                if n >= 2:
                    pe.wait_ge(spr_out, n - 1)
                for half in range(2):
                    cols = slice(half * HALF, (half + 1) * HALF)
                    ins = pe.matmul(PS[n % 2][:, cols], spread[0:8, pair, :], alpha_st[:, g, cols], start=True, stop=True)
                ins.then_inc(spr_done, 1)
            pe.wait_ge(spr_out, 5)
            pe.wait_ge(fbias_ok, 1)

            mixer_steps(STEPS * N_DIL, STEPS * MIX)

            pe.wait_ge(exp_done, STEPS * MIX)
            pe.wait_ge(pt_lo, units_before(STEPS * MIX))
            pe.wait_ge(ote_done, 8 * MIX)
            def branches(c):
                split_products(PS[2], w_of(c), lambda part, k: br_in[:, part, k, :], 4)
                split_products(PS[3], lambda part, k: wsp[:, c % 2, part, (4 + k) * P:(5 + k) * P],
                               lambda part, k: br_in[:, part, 4 + k, :], 2).then_inc(w_used, 1)

            C = CH0 + 3 * MIX
            pe.wait_ge(w_lo, C + 3)
            split_products(PS[0], w_of(C + 2), h_at, KC).then_inc(w_used, 1)
            pe.wait_ge(w_lo, C + 4)
            pe.wait_ge(br_lo, 6)
            pe.wait_ge(raw_out, 6 * MIX + 4)
            branches(C + 3)
            pe.wait_ge(w_lo, C + 5)
            split_products(PS[1], w_of(C + 4), h_at, KC).then_inc(w_used, 1)
            pe.wait_ge(w_lo, C + 6)
            pe.wait_ge(gmul, 2 + PRIME)
            branches(C + 5)
            with pe.Fori(1, N_GATE // 2) as it:
                for n in range(6):
                    m, j = divmod(n, 3)
                    c = CH0 + 3 * MIX + n
                    if j < 2:
                        pe.wait_ge(sig_ok, it * 4 + 2 * m + PRIME)
                        pe.wait_ge(w_lo, it * 6 + (c + 1))
                        split_products(PS[j], w_of(c), h_at, KC).then_inc(w_used, 1)
                    else:
                        pe.wait_ge(gmul, it * 4 + 2 * m + PRIME)
                        pe.wait_ge(w_lo, it * 6 + (c + 1))
                        branches(c)

            def ring_w(n):
                return lambda part, k: wsp_at(n, part)[:, k * P:(k + 1) * P]

            def x_chunk(n):
                pe.wait_ge(xcol_in[n % 2], 16 * (n // 2 + 1))
                if n < 2:
                    pe.wait_ge(gmul, 2 * N_GATE + PRIME)
                else:
                    pe.wait_ge(xres, n - 1)
                for t in range(8):
                    ins = pe.transpose(PS[2 + n % 2][:, t * P:(t + 1) * P], tmp[:, 5 + n % 2, t * P:(t + 1) * P],
                                       ident[:])
                ins.then_inc(xct_done, 1)

            pe.wait_ge(sig_ok, 2 * N_GATE + PRIME)
            for n in range(KC):
                if n >= 1:
                    x_chunk(n)
                pe.wait_ge(w_lo, CH_OUT + n + 1)
                if n >= 2:
                    pe.wait_ge(resid, n - 1)
                if n == 0:
                    products_by_chunk(PS[0], ring_w(0), h_at, m_lo, 0).then_inc(w_used, 1)
                    x_chunk(0)
                else:
                    split_products(PS[n % 2], ring_w(n), h_at, KC).then_inc(w_used, 1)

            def mean_square():
                pe.wait_ge(acc_ok, KC + 1)
                pe.wait_ge(xres, KC)
                for half in range(2):
                    cols = slice(half * HALF, (half + 1) * HALF)
                    ins = pe.matmul(PS[2][:, cols], mean_w[:], tmp[:, 3, cols], start=True, stop=True)
                ins.then_inc(mean_done, 1)

            def mlp_block(b, first):
                for j in range(4):
                    if first:
                        if j < 2:
                            pe.wait_ge(resid, KC - 1 + j)
                        else:
                            pe.wait_ge(u_r, j - 1 + PRIME)
                    else:
                        pe.wait_ge(u_r, b * 4 + (max(j - 1, 0) + PRIME))
                    pe.wait_ge(w_lo, b * 8 + (CH_OUT + KC + j + 1))
                    if first and j == 0:
                        products_by_chunk(PS[0], ring_w(0), mlp_in, h_lo, 0).then_inc(w_used, 1)
                        mean_square()
                    else:
                        split_products(PS[j % 2], ring_w(j), mlp_in, KC).then_inc(w_used, 1)
                if first:
                    pe.wait_ge(mean_out, 1)
                for m, hidden in [(0, (0, 1, 2)), (1, (0, 1, 2)), (0, (3,)), (1, (3,))] + [(m, (0, 1, 2, 3))
                                                                                      for m in range(2, 8)]:
                    if hidden[0] == 0:
                        if m % 2 == 0:
                            pe.wait_ge(w_lo, b * 8 + (CH_OUT + KC + 4 + m // 2 + 1))
                        if m < 2:
                            pe.wait_ge(dn_add, b * 8 + PRIME)
                        else:
                            pe.wait_ge(dn_add, b * 8 + (m - 1) + PRIME)
                    if m == 0:
                        pe.wait_ge(u_lo, b * 4 + (hidden[-1] + 1) + PRIME)
                    for half in range(2):
                        cols = slice(half * HALF, (half + 1) * HALF)
                        for f in hidden:
                            for n, (wp, mp) in enumerate(((0, 0), (0, 1), (1, 0))):
                                a = f * 256 + (m % 2) * P
                                ins = pe.matmul(PS[2 + m % 2][:, cols], wsp_at(m // 2, wp)[:, a:a + P],
                                                hid[:, mp, f, cols], start=(f == 0 and n == 0),
                                                stop=(f == 3 and n == 2), skip_group_check=True)
                    if hidden[-1] == 3:
                        ins.then_inc(w_used if m % 2 else dn_even, 1)

            mlp_block(0, True)
            with pe.Fori(1, FF_BLOCKS) as b:
                mlp_block(b, False)

            pe.wait_ge(facc, KC)
            for i in range(8):
                ins = pe.matmul(PS[0][:, i:i + 1], tmp[:, 3, i * P:(i + 1) * P], mean_w[:, 0:1], start=True, stop=True)
            ins.then_inc(fmean, 1)
            for i in range(8):
                if i >= 3:
                    pe.wait_ge(y_ok, i - 2)
                for c in range(KC):
                    ins = pe.transpose(PS[1 + i % 3][:, c * P:(c + 1) * P], kp[:, c, i * P:(i + 1) * P], ident[:])
                ins.then_inc(ft_done, 1)

        @block.scalar
        def _(act):
            for primed in (sig_ok, u_sq):
                act.sem_inc(primed, 1)
            chain = [0]

            def link(ins):
                chain[0] += 1
                ins.then_inc(achain, 1)
                act.wait_ge(achain, chain[0])

            def split_hi(c):
                act.wait_ge(w_in_s[c % 2], 16 * (c // 2 + 1))
                after(act, w_used, c - 1)
                act.copy(wsp[:, c % 2, 0, :], raw[:, c % 2, :]).then_inc(w_hi, 1)

            def square(i):
                act.wait_ge(x_in[i], 16)
                after(act, x_sq, i)
                act.activation(PS[3][:], x_tile(i), ACT.Square, accum_out=xstat[:, i:i + 1]).then_inc(x_sq, 1)

            def root(half):
                act.wait_ge(x_st, half + 1)
                act.activation(xstat[:, 4 * half:4 * half + 4], xstat[:, 4 * half:4 * half + 4],
                               ACT.Sqrt).then_inc(x_root, 1)

            def x_hi(half, c):
                n = half * KC + c
                act.wait_ge(xt_done, n + 1)
                bank = PS[(n % 4) // 2][:, (n % 2) * HALF:(n % 2 + 1) * HALF]
                act.activation(hspl[:, 0, c, half * HALF:(half + 1) * HALF], bank, ACT.Copy,
                               scale=ga_g[:, c:c + 1]).then_inc(xhi, 1)

            for i in range(4):
                square(i)
            root(0)
            square(4)
            split_hi(0)
            act.wait_ge(small_in, 48)
            for c in range(4):
                x_hi(0, c)
            square(5)
            for c in range(4, KC):
                x_hi(0, c)
            square(6)
            square(7)
            root(1)
            split_hi(1)
            for c in range(KC):
                x_hi(1, c)
            act.wait_ge(consts, N_CONST)
            act.copy(spread[:], spread_f[:]).then_inc(spread_ok, 1)
            split_hi(2)
            act.wait_ge(fz_ok, 1)
            fz, fe = forget[:2]
            link(act.activation(fe, fz, ACT.Abs))
            link(act.activation(fe, fe, ACT.Exp, scale=-1.0))
            act.activation(fe, fe, ACT.Ln, bias=1.0).then_inc(fln_ok, 1)

            def group_wait(u, g):
                if g % 2:
                    act.wait_ge(w_used, CH0 + 3 * u + g // 2 + 1)
                else:
                    act.wait_ge(half_done, 3 * u + g // 2 + 1)

            def raw_evacuate(u, g):
                group_wait(u, g)
                if g == 0:
                    after(act, k_lo, 2 * u)
                elif g == 2:
                    after(act, q_lo, 2 * STEPS * (u - 1))
                elif g == 4:
                    after(act, vt_done, 2 * u)
                    if u < N_DIL:
                        act.wait_ge(roped, 16 * u + 16)
                half = g % 2
                if g < 4:
                    dst = (k_raw if g < 2 else q_raw(u))[:, half * HALF:(half + 1) * HALF]
                    src = psp(u, g)
                else:
                    d = dil_of(u) or 1
                    n = HALF // d
                    dst = v_raw.rearrange("p (r l) -> p r l", r=d)[:, :, half * n:(half + 1) * n]
                    src = psp(u, g).rearrange("p (l r) -> p r l", r=d)
                act.copy(dst, src).then_inc(raw_out, 1)

            def k_stack(u, h):
                act.wait_ge(raw_out, 6 * u + 2)
                if u < N_DIL:
                    act.wait_ge(roped, 16 * u + 8)
                after(act, qk_done, STEPS * (u - 1))
                row = 64 * h
                act.copy(ordered(k_st[u % 2][h][row:row + 64], u), natural(k_raw[row:row + 64], u)).then_inc(k_hi, 1)

            def q_tile(G):
                t, s = divmod(G, STEPS)
                act.wait_ge(raw_out, 6 * t + 4)
                if t < N_DIL:
                    act.wait_ge(roped, 16 * t + 16)
                after(act, qk_done, G - 2)
                row = 64 * (s % 2)
                for dst in (0, 64):
                    act.activation(tile_view(q_st[dst:dst + 64, G % 3, 0, :], t),
                                   tile_tokens(q_raw(t)[row:row + 64], t, s // 2), ACT.Copy,
                                   scale=QSCALE).then_inc(q_hi, 1)

            def values_hi(t):
                for bank in range(2):
                    act.wait_ge(vt_done, 2 * t + bank + 1)
                    after(act, pv_done, STEPS * t)
                    act.copy(v_nat[:, 4 * bank:4 * bank + 4, :, 0, :],
                             PS[2][:, bank * HALF:(bank + 1) * HALF].rearrange("p (t h d) -> p t h d", t=4, h=2)
                             ).then_inc(v_hi, 1)

            def exps(G):
                n = len(tiles_of(G))
                c = column(G)
                act.wait_ge(max_done, G + 1)
                after(act, tr_done, units_before(G - 1))
                act.activation(probs(G)[:, 0:n * P], psc[G % 2][:, 0:n * P], ACT.Exp,
                               bias=negmax[:, c:c + 1], accum_out=rowsum[:, c:c + 1]).then_inc(exp_done, 1)

            def probs_hi(G):
                for n, (a, b) in enumerate(units_of(G)):
                    u = units_before(G) + n
                    act.wait_ge(tr_done, u + 1)
                    after(act, pv_done, G - 1)
                    act.copy(pt[:, G % 2, 0, a * P:b * P],
                             PS[2][:, (u % 2) * HALF:(u % 2) * HALF + (b - a) * P]).then_inc(pt_hi, 1)

            def out_part(G):
                c = column(G)
                act.wait_ge(pv_done, G + 1)
                act.wait_ge(inv_done, G + 1)
                after(act, on_done, G - 1)
                act.activation(o_part[:, G % 2, :], pso[:, (G % 2) * P + HD:(G % 2 + 1) * P], ACT.Copy,
                               scale=rowinv[:, c:c + 1]).then_inc(op_done, 1)

            def out_store(i):
                act.wait_ge(ot_done, i + 1)
                if i == 8 * N_DIL:
                    act.wait_ge(comb_ok, 1)
                act.wait_ge(pv_done, min(2 * i + 3, STEPS * (N_DIL if i < 8 * N_DIL else MIX)))
                t, tile = divmod(i, 8)
                if t < N_DIL:
                    dst = tile_tokens(og[:, t // 2, (t % 2) * 1024:(t % 2 + 1) * 1024], t, tile)
                else:
                    dst = keep[:, (t - N_DIL) * 1024 + tile * P:(t - N_DIL) * 1024 + (tile + 1) * P]
                act.copy(dst, tile_view(pso[:, 256:256 + P], t)).then_inc(ote_done, 1)

            def mixer_steps(first, last):
                for G in range(first, last + 4):
                    t, s = divmod(G, STEPS)
                    if group_out(t, s) is not None and G < last:
                        raw_evacuate(t + 1, group_out(t, s))
                    if s == 0 and G > first:
                        raw_evacuate(t, 5 if t < MIX else 3)
                    if G % 2 and G - 5 >= first:
                        out_store((G - 5) // 2)
                    if first <= G - 3 < last:
                        out_part(G - 3)
                    if G < last and G + 2 < STEPS * MIX:
                        q_tile(G + 2)
                    if G < last:
                        exps(G)
                    if first <= G - 1 < last:
                        probs_hi(G - 1)
                    if G < last:
                        if s == 1:
                            values_hi(t)
                        if s == (0 if t == N_DIL else 2):
                            split_hi(CH0 + 3 * t + 4)
                        if t == MIX - 1 and s == 9:
                            split_hi(CH0 + 3 * t + 5)
                        if t + 1 < MIX:
                            if s == 7:
                                split_hi(CH0 + 3 * t + 5)
                            if s in (8, 9):
                                k_stack(t + 1, s - 8)
                            if s == 13:
                                split_hi(CH0 + 3 * t + 6)

            raw_evacuate(0, 0)
            raw_evacuate(0, 1)
            split_hi(3)
            raw_evacuate(0, 2)
            k_stack(0, 0)
            k_stack(0, 1)
            raw_evacuate(0, 3)
            split_hi(4)
            raw_evacuate(0, 4)
            q_tile(0)
            q_tile(1)
            raw_evacuate(0, 5)
            mixer_steps(0, STEPS * N_DIL)

            act.wait_ge(exp_done, STEPS * N_DIL)
            act.wait_ge(inv_done, STEPS * N_DIL)
            act.activation(rowsum[:, 0:96], rowsum[:, 0:96], ACT.Ln).then_inc(ln_ok, 1)
            to_natural(1, lambda dst, src: act.copy(dst, src), act)
            raw_evacuate(N_DIL + 1, 0)
            act.wait_ge(lsub_ok, 1)
            act.activation(lse_nat, lse_nat, ACT.Exp).then_inc(lexp_ok, 1)
            act.wait_ge(alpha_f, 1)
            act.copy(alpha_nat[:, :, :, 0, :], lse_nat.rearrange("p g (i h) -> p g i h", i=8)).then_inc(alpha_hi, 1)
            for g in (1, 2):
                act.wait_ge(at_done, 3)
                act.copy(alpha_st[:, g, :], PS[g][0:8, :]).then_inc(alpha_row[g], 1)
            raw_evacuate(N_DIL + 1, 1)
            mixer_steps(STEPS * N_DIL, STEPS * MIX)

            act.wait_ge(pv_done, STEPS * MIX)
            act.wait_ge(ote_done, 8 * MIX)
            for k in range(6):
                src = keep[:, k * 1024:(k + 1) * 1024] if k < 4 else ob[:, (k - 4) * 1024:(k - 3) * 1024]
                act.copy(br_in[:, 0, k, :], src).then_inc(br_hi, 1)
            C = CH0 + 3 * MIX
            split_hi(C + 3)
            act.wait_ge(raw_out, 6 * MIX + 4)
            for x in gate0:
                act.activation(x, x, ACT.Sigmoid).then_inc(sig_ok, 1)
            for n, gate in ((2, 0), (3, None), (4, 1), (5, None)):
                act.wait_ge(w_used, C + n + 1)
                if gate is not None:
                    act.activation(tmp[:, gate, :], PS[gate][:], ACT.Sigmoid).then_inc(sig_ok, 1)
                split_hi(C + n + 2)

            def gates(it, last):
                for n in range(6):
                    m, j = divmod(n, 3)
                    c = CH0 + 3 * MIX + n
                    if j < 2:
                        act.wait_ge(w_used, it * 6 + (c + 1))
                        act.wait_ge(mixed_ok, it * 2 + m + PRIME)
                        act.activation(tmp[:, j, :], PS[j][:], ACT.Sigmoid).then_inc(sig_ok, 1)
                    if last and n == 5:
                        for k in range(KC - 1):
                            act.wait_ge(mixed_ok, k + 1 + PRIME)
                            act.copy(hspl[:, 0, k, :], kp[:, k, :]).then_inc(m_hi, 1)
                    act.wait_ge(w_in_s[c % 2], it * 48 + 16 * ((c + 2) // 2 + 1))
                    act.wait_ge(w_used, it * 6 + (c + 1))
                    act.copy(wsp[:, c % 2, 0, :], raw[:, c % 2, :]).then_inc(w_hi, 1)

            with act.Fori(1, N_GATE // 2 - 1) as it:
                gates(it, False)
            gates(N_GATE // 2 - 1, True)
            act.wait_ge(mixed_ok, KC + PRIME)
            act.copy(hspl[:, 0, KC - 1, :], kp[:, KC - 1, :]).then_inc(m_hi, 1)

            def split_hi2(n, b=None):
                loaded, count = loaded_at(n)
                if b is None:
                    act.wait_ge(loaded, 16 * count)
                    act.wait_ge(w_used, CH_OUT + max(n - 3, 0))
                else:
                    act.wait_ge(loaded, b * 32 + 16 * count)
                    act.wait_ge(w_used, b * 8 + (CH_OUT + n - 3))
                act.copy(wsp_at(n, 0), raw_at(n)).then_inc(w_hi, 1)

            def mlp_in_hi(c):
                act.wait_ge(resid, c + 1)
                act.activation(mlp_in(0, c), kp[:, c, :], ACT.Copy, scale=gm_g[:, c:c + 1]).then_inc(h_hi, 1)

            split_hi2(2)
            for n in range(KC):
                split_hi2(n + 3)
                act.wait_ge(xct_done, n + 1)
                act.wait_ge(m_lo, n + 1)
                act.copy(kp[:, n, :], PS[2 + n % 2][:]).then_inc(xres, 1)
                if n == KC - 1:
                    act.wait_ge(w_used, CH_OUT + KC)
                    for c in range(4, KC - 1):
                        mlp_in_hi(c)
                act.wait_ge(resid, n + 1)
                if n < 4 or n == KC - 1:
                    mlp_in_hi(n)
                if n >= 1:
                    act.wait_ge(acc_ok, n + 1)
                act.activation(tmp[:, 1, :], kp[:, n, :], ACT.Square).then_inc(sq_ok, 1)
            act.wait_ge(mean_done, 1)
            act.wait_ge(acc_ok, KC + 1)
            act.activation(tmp[:, 1, :], PS[2][:], ACT.Sqrt, bias=eps_c[:]).then_inc(mean_out, 1)

            def mlp_block(b, last):
                for j in range(4):
                    split_hi2(KC + j + 3, b)
                    act.wait_ge(u_r, b * 4 + (j + 1) + PRIME)
                    act.wait_ge(u_lo, b * 4 + j + PRIME)
                    act.wait_ge(rstd_ok, 1)
                    act.activation(tmp[:, 1, :], tmp[:, 0, :], ACT.Square).then_inc(u_sq, 1)
                    act.wait_ge(u_sq, b * 4 + (j + 1) + PRIME)
                    act.wait_ge(w_used, b * 8 + (CH_OUT + KC))
                    act.copy(hid[:, 0, j, :], tmp[:, 1, :]).then_inc(u_hi, 1)
                for j in range(4, 8):
                    if not last or j + 3 < 8:
                        split_hi2(KC + j + 3, b)
                    if last:
                        if j == 4:
                            act.wait_ge(u_sq, FF_BLOCKS * 4 + PRIME)
                        for m in (2 * j - 8, 2 * j - 7):
                            act.wait_ge(dn_add, b * 8 + (m + 1) + PRIME)
                            if m >= 1:
                                act.wait_ge(facc, m)
                            act.activation(tmp[:, 0, :], kp[:, m, :], ACT.Square).then_inc(fsq, 1)

            with act.Fori(0, FF_BLOCKS - 1) as b:
                mlp_block(b, False)
            mlp_block(FF_BLOCKS - 1, True)
            act.wait_ge(fmean_out, 1)
            act.activation(xstat[:], xstat[:], ACT.Sqrt).then_inc(froot, 1)

        @block.vector
        def _(dve):
            for primed in (gmul, mixed_ok, u_r, u_lo, dn_add):
                dve.sem_inc(primed, 1)
            chain = [0]

            def link(ins):
                chain[0] += 1
                ins.then_inc(dchain, 1)
                dve.wait_ge(dchain, chain[0])

            def split_lo(c, half=None):
                cols = slice(0, 1024) if half is None else slice(half * HALF, (half + 1) * HALF)
                dve.wait_ge(w_hi, c + 1)
                ins = dve.tensor_tensor(wsp[:, c % 2, 1, cols], raw[:, c % 2, cols],
                                        wsp[:, c % 2, 0, cols].bitcast(F32), ALU.subtract)
                if half != 0:
                    ins.then_inc(w_lo, 1)

            for half in range(2):
                h4 = slice(4 * half, 4 * half + 4)
                dve.wait_ge(x_sq, 4 * half + 4)
                dve.tensor_scalar(xstat[:, h4], xstat[:, h4], 1.0 / D, EPS, ALU.mult, ALU.add).then_inc(x_st, 1)
                dve.wait_ge(x_root, half + 1)
                dve.reciprocal(xrstd[:, h4], xstat[:, h4]).then_inc(x_rs, 1)
                dve.wait_ge(x_rs, half + 1)
                for i in range(4):
                    t = 4 * half + i
                    dve.tensor_scalar(x_tile(t), x_tile(t), xrstd[:, t:t + 1], None, ALU.mult).then_inc(x_scaled, 1)
                if half == 0:
                    split_lo(0)
                else:
                    split_lo(1)
                for c in range(KC):
                    n = half * KC + c
                    dve.wait_ge(xhi, n + 1)
                    bank = PS[(n % 4) // 2][:, (n % 2) * HALF:(n % 2 + 1) * HALF]
                    cols = slice(half * HALF, (half + 1) * HALF)
                    dve.scalar_tensor_tensor(out=hspl[:, 1, c, cols], in0=bank, scalar=ga_g[:, c:c + 1],
                                             in1=hspl[:, 0, c, cols].bitcast(F32), op0=ALU.mult,
                                             op1=ALU.subtract).then_inc(xlo, 1)
            H8 = FOX_HEADS
            fz, fe, fc, fo = forget
            mid = fe[:, 0:512].bitcast(BF16)
            dve.wait_ge(w_used, 1)
            dve.wait_ge(xt_done, 16)
            dve.wait_ge(small_in, 48)
            dve.tensor_scalar(fz, PS[2][0:H8, :], bfor[0:H8, :], None, ALU.add).then_inc(fz_ok, 1)
            split_lo(2)
            link(dve.memset(fo, 1.0))
            dve.wait_ge(fln_ok, 1)
            dve.wait_ge(fz_ok, 1)
            link(dve.scalar_tensor_tensor(out=fz, in0=fz, scalar=0.0, in1=fe, op0=ALU.min, op1=ALU.subtract))
            link(dve.tensor_tensor_scan(fc, fo, fz, 0.0, ALU.mult, ALU.add))
            dve.wait_ge(consts, N_CONST)
            link(dve.tensor_scalar(fbias[0:H8, :], fc, -1.0, None, ALU.mult))
            link(dve.scalar_tensor_tensor(out=fz, in0=fc, scalar=-1.0, in1=fbias[0:H8, :], op0=ALU.mult,
                                          op1=ALU.subtract))
            link(dve.tensor_copy(mid, fz))
            dve.tensor_copy(fbias[32:32 + H8, :], fz)
            link(dve.tensor_tensor(fz, fz, mid, ALU.subtract))
            dve.tensor_copy(fbias[64:64 + H8, :], fz).then_inc(fbias_ok, 1)
            dve.wait_ge(fbias_ok, 1)

            def rotate(u, which, half, n):
                cols = slice(half * HALF, (half + 1) * HALF)
                x = (k_raw, q_raw(u))[which][:, cols]
                other = v_raw[:, cols]
                if n == 0:
                    dve.wait_ge(raw_out, 6 * u + 2 * which + half + 1)
                    dve.wait_ge(rope_in, 16)
                    after(dve, vt_done, 2 * u)
                    swap = list(range(8, 16)) + list(range(8)) + list(range(16, 32))
                    ins = dve.stream_shuffle(other, x, swap)
                else:
                    dve.wait_ge(roped, 16 * u + 8 * which + 4 * half + n)
                    if n == 1:
                        ins = dve.tensor_tensor(x, x, rope_c[:, cols], ALU.mult)
                    elif n == 2:
                        ins = dve.tensor_tensor(other, other, rope_s[:, cols], ALU.mult)
                    else:
                        ins = dve.tensor_tensor(x, x, other, ALU.add)
                ins.then_inc(roped, 1)

            def k_stack(u, h):
                row = 64 * h
                dve.wait_ge(k_hi, 2 * u + h + 1)
                dve.tensor_tensor(ordered(k_st[u % 2][h][64 - row:P - row], u), natural(k_raw[row:row + 64], u),
                                  ordered(k_st[u % 2][h][row:row + 64].bitcast(F32), u), ALU.subtract).then_inc(k_lo, 1)

            def q_tile(G):
                t, s = divmod(G, STEPS)
                row = 64 * (s % 2)
                dve.wait_ge(q_hi, 2 * G + 2)
                for dst in (0, 64):
                    dve.scalar_tensor_tensor(out=tile_view(q_st[dst:dst + 64, G % 3, 1, :], t),
                                             in0=tile_tokens(q_raw(t)[row:row + 64], t, s // 2), scalar=QSCALE,
                                             in1=tile_view(q_st[row:row + 64, G % 3, 0, :].bitcast(F32), t),
                                             op0=ALU.mult, op1=ALU.subtract).then_inc(q_lo, 1)

            def values_lo(t):
                for bank in range(2):
                    dve.wait_ge(v_hi, 2 * t + bank + 1)
                    dve.tensor_tensor(v_nat[:, 4 * bank:4 * bank + 4, :, 1, :],
                                      PS[2][:, bank * HALF:(bank + 1) * HALF].rearrange("p (t h d) -> p t h d", t=4, h=2),
                                      v_nat[:, 4 * bank:4 * bank + 4, :, 0, :].bitcast(F32),
                                      ALU.subtract).then_inc(v_lo, 1)

            def maxes(G):
                n = len(tiles_of(G))
                c = column(G)
                dve.wait_ge(qk_done, G + 1)
                dve.tensor_reduce(negmax[:, c:c + 1], psc[G % 2][:, 0:n * P], AX_X, ALU.max,
                                  negate=True).then_inc(max_done, 1)

            def probs_lo(G):
                for n, (a, b) in enumerate(units_of(G)):
                    u = units_before(G) + n
                    dve.wait_ge(pt_hi, u + 1)
                    dve.tensor_tensor(pt[:, G % 2, 1, a * P:b * P],
                                      PS[2][:, (u % 2) * HALF:(u % 2) * HALF + (b - a) * P],
                                      pt[:, G % 2, 0, a * P:b * P].bitcast(F32), ALU.subtract).then_inc(pt_lo, 1)

            def inverses(G):
                c = column(G)
                dve.wait_ge(exp_done, G + 1)
                dve.reciprocal(rowinv[:, c:c + 1], rowsum[:, c:c + 1]).then_inc(inv_done, 1)

            def outs(G):
                i, h = divmod(G, 2)
                c = column(G)
                dve.wait_ge(op_done, G + 1)
                dve.wait_ge(inv_done, G + 1)
                after(dve, ot_done, i - 1)
                dve.scalar_tensor_tensor(out=o_nat[:, i % 2, h * HD:(h + 1) * HD],
                                         in0=pso[:, h * P:h * P + HD], scalar=rowinv[:, c:c + 1],
                                         in1=o_part[:, h, :], op0=ALU.mult, op1=ALU.add).then_inc(on_done, 1)

            def side_work(G):
                t, s = divmod(G, STEPS)
                u = t + 1
                jobs = []
                if t == MIX - 1 and s == 10:
                    jobs += [lambda: split_lo(CH0 + 3 * t + 5, 0), lambda: split_lo(CH0 + 3 * t + 5, 1)]
                for s0, s1, c in ((1, 1, 3 * t + 4) if t == N_DIL else (3, 4, 3 * t + 4), (8, 8, 3 * t + 5),
                                  (14, 14, 3 * t + 6)):
                    if u < MIX or c == 3 * t + 4:
                        jobs += [lambda c=c: split_lo(CH0 + c, 0)] if s == s0 else []
                        jobs += [lambda c=c: split_lo(CH0 + c, 1)] if s == s1 else []
                if u < MIX and s in (9, 15):
                    jobs.append(lambda: k_stack(u, (s - 9) // 6))
                if u < N_DIL:
                    jobs += [lambda n=n: rotate(u, n // 8, n // 4 % 2, n % 4) for n in ROTATE_OPS.get(s, ())]
                return jobs

            def mixer_steps(first, last):
                for G in range(first, last + 3):
                    t, s = divmod(G, STEPS)
                    if first <= G - 3 < last:
                        outs(G - 3)
                    jobs = side_work(G) if G < last else []
                    if G < last:
                        maxes(G)
                    for job in jobs[:1]:
                        job()
                    if first <= G - 1 < last:
                        probs_lo(G - 1)
                        inverses(G - 1)
                    if G < last and G + 2 < STEPS * MIX:
                        q_tile(G + 2)
                    if s == 1 and G < last:
                        values_lo(t)
                    for job in jobs[1:]:
                        job()

            for n in range(8):
                rotate(0, 0, n // 4, n % 4)
            split_lo(3)
            k_stack(0, 0)
            k_stack(0, 1)
            for n in range(8):
                rotate(0, 1, n // 4, n % 4)
            split_lo(4)
            q_tile(0)
            q_tile(1)
            mixer_steps(0, STEPS * N_DIL)

            dve.wait_ge(ln_ok, 1)
            dve.tensor_tensor(rowsum[:, 0:96], rowsum[:, 0:96], negmax[:, 0:96], ALU.subtract).then_inc(lse_ok, 1)
            for g in (0, 2):
                to_natural(g, lambda dst, src: dve.tensor_copy(dst, src), dve)
            dve.wait_ge(ln_done, 1)
            link(dve.tensor_copy(lse_nat, pso[:, 0:96].rearrange("p (g c) -> p g c", g=3)))
            link(dve.tensor_tensor(top, lse_nat[:, 0, :], lse_nat[:, 1, :], ALU.max))
            link(dve.tensor_tensor(top, top, lse_nat[:, 2, :], ALU.max))
            for g in range(3):
                ins = dve.tensor_tensor(lse_nat[:, g, :], lse_nat[:, g, :], top, ALU.subtract)
            ins.then_inc(lsub_ok, 1)
            dve.wait_ge(lexp_ok, 1)
            link(dve.tensor_tensor(top, lse_nat[:, 0, :], lse_nat[:, 1, :], ALU.add))
            link(dve.tensor_tensor(top, top, lse_nat[:, 2, :], ALU.add))
            link(dve.reciprocal(top, top))
            for g in range(3):
                ins = dve.tensor_tensor(lse_nat[:, g, :], lse_nat[:, g, :], top, ALU.mult)
            ins.then_inc(alpha_f, 1)
            dve.wait_ge(alpha_f, 1)
            dve.wait_ge(alpha_hi, 1)
            dve.tensor_tensor(alpha_nat[:, :, :, 1, :], lse_nat.rearrange("p g (i h) -> p g i h", i=8),
                              alpha_nat[:, :, :, 0, :].bitcast(F32), ALU.subtract).then_inc(alpha_lo, 1)
            dve.wait_ge(at_done, 3)
            dve.tensor_copy(alpha_st[:, 0, :], PS[0][0:8, :]).then_inc(alpha_row[0], 1)
            dve.wait_ge(ote_done, 8 * N_DIL)
            for n in range(6):
                g, pair = divmod(n, 2)
                dve.wait_ge(spr_done, n + 1)
                dst = ob[:, pair * 1024:(pair + 1) * 1024]
                one = dst if g == 0 else tmp[:, 6, :]
                dve.tensor_tensor(one, PS[pair][:], og[:, g, pair * 1024:(pair + 1) * 1024], ALU.mult).then_inc(spr_out, 1)
                if g > 0:
                    dve.wait_ge(spr_out, n + 1)
                    ins = dve.tensor_tensor(dst, dst, one, ALU.add)
                    if n < 5:
                        link(ins)
                    else:
                        ins.then_inc(comb_ok, 1)
            mixer_steps(STEPS * N_DIL, STEPS * MIX)

            for k in range(6):
                src = keep[:, k * 1024:(k + 1) * 1024] if k < 4 else ob[:, (k - 4) * 1024:(k - 3) * 1024]
                dve.wait_ge(br_hi, k + 1)
                dve.tensor_tensor(br_in[:, 1, k, :], src, br_in[:, 0, k, :].bitcast(F32), ALU.subtract).then_inc(br_lo, 1)
            C = CH0 + 3 * MIX
            split_lo(C + 3)
            for n in range(2, 6):
                if n in (3, 5):
                    m = n // 4
                    pair = (gate0, (tmp[:, 0, :], tmp[:, 1, :]))[m]
                    dve.wait_ge(w_used, C + n + 1)
                    dve.wait_ge(sig_ok, 2 * m + 2 + PRIME)
                    for a in range(2):
                        dve.tensor_tensor(pair[a], pair[a], PS[2 + a][:], ALU.mult).then_inc(gmul, 1)
                    dve.wait_ge(gmul, 2 * m + 2 + PRIME)
                    dve.tensor_tensor(kp[:, m, :], pair[0], pair[1], ALU.add).then_inc(mixed_ok, 1)
                split_lo(C + n + 2)
            def mixed_lo(c):
                dve.wait_ge(m_hi, c + 1)
                dve.tensor_tensor(hspl[:, 1, c, :], kp[:, c, :], hspl[:, 0, c, :].bitcast(F32), ALU.subtract).then_inc(m_lo, 1)

            def gates(it, last):
                for n in range(6):
                    m, j = divmod(n, 3)
                    c = CH0 + 3 * MIX + n
                    if last and n == 5:
                        for k in range(KC - 1):
                            mixed_lo(k)
                    if j == 2:
                        dve.wait_ge(w_used, it * 6 + (c + 1))
                        for a in range(2):
                            dve.wait_ge(sig_ok, it * 4 + (2 * m + a + 1) + PRIME)
                            dve.tensor_tensor(tmp[:, a, :], tmp[:, a, :], PS[2 + a][:], ALU.mult).then_inc(gmul, 1)
                        dve.wait_ge(gmul, it * 4 + (2 * m + 2) + PRIME)
                        a0 = it * 2048 + m * 1024
                        dve.tensor_tensor(keep[:, a0:a0 + 1024] if last else keep[:, bass.ds(a0, 1024)], tmp[:, 0, :], tmp[:, 1, :],
                                          ALU.add).then_inc(mixed_ok, 1)
                    dve.wait_ge(w_hi, it * 6 + (c + 3))
                    dve.tensor_tensor(wsp[:, c % 2, 1, :], raw[:, c % 2, :], wsp[:, c % 2, 0, :].bitcast(F32),
                                      ALU.subtract).then_inc(w_lo, 1)

            with dve.Fori(1, N_GATE // 2 - 1) as it:
                gates(it, False)
            gates(N_GATE // 2 - 1, True)
            mixed_lo(KC - 1)

            def split_lo2(n, b=0):
                dve.wait_ge(w_hi, b * 8 + (CH_OUT + n + 1))
                dve.tensor_tensor(wsp_at(n, 1), raw_at(n), wsp_at(n, 0).bitcast(F32), ALU.subtract).then_inc(w_lo, 1)

            dve.memset(tmp[:, 3, :], 0.0).then_inc(acc_ok, 1)
            split_lo2(2)
            for n in range(KC):
                split_lo2(n + 3)
                dve.wait_ge(w_used, CH_OUT + n + 1)
                dve.wait_ge(xres, n + 1)
                dve.tensor_tensor(kp[:, n, :], kp[:, n, :], PS[n % 2][:], ALU.add).then_inc(resid, 1)
                for c in (n,) if n < 4 else (4, 5, 6, 7) if n == KC - 1 else ():
                    dve.wait_ge(h_hi, c + 1)
                    dve.scalar_tensor_tensor(out=mlp_in(1, c), in0=kp[:, c, :], scalar=gm_g[:, c:c + 1],
                                             in1=mlp_in(0, c).bitcast(F32), op0=ALU.mult,
                                             op1=ALU.subtract).then_inc(h_lo, 1)
                dve.wait_ge(sq_ok, n + 1)
                dve.wait_ge(acc_ok, n + 1)
                dve.tensor_tensor(tmp[:, 3, :], tmp[:, 3, :], tmp[:, 1, :], ALU.add).then_inc(acc_ok, 1)
            dve.wait_ge(mean_out, 1)
            dve.reciprocal(tmp[:, 3, :], tmp[:, 1, :]).then_inc(rstd_ok, 1)
            dve.wait_ge(rstd_ok, 1)

            def mlp_block(b, last):
                for j in range(4):
                    split_lo2(KC + j + 3, b)
                    dve.wait_ge(w_used, b * 8 + (CH_OUT + KC + j + 1))
                    dve.wait_ge(u_sq, b * 4 + j + PRIME)
                    dve.scalar_tensor_tensor(out=tmp[:, 0, :], in0=PS[j % 2][:], scalar=0.0, in1=tmp[:, 3, :],
                                             op0=ALU.max, op1=ALU.mult).then_inc(u_r, 1)
                    dve.wait_ge(u_hi, b * 4 + (j + 1))
                    dve.tensor_tensor(hid[:, 1, j, :], tmp[:, 1, :], hid[:, 0, j, :].bitcast(F32),
                                      ALU.subtract).then_inc(u_lo, 1)
                if last:
                    link(dve.memset(tmp[:, 3, :], 0.0))
                for j in range(4, 8):
                    if not last or j + 3 < 8:
                        split_lo2(KC + j + 3, b)
                    for m in (2 * j - 8, 2 * j - 7):
                        if m % 2:
                            dve.wait_ge(w_used, b * 8 + (CH_OUT + KC + 4 + m // 2 + 1))
                        else:
                            dve.wait_ge(dn_even, b * 4 + (m // 2 + 1))
                        dve.tensor_tensor(kp[:, m, :], kp[:, m, :], PS[2 + m % 2][:], ALU.add).then_inc(dn_add, 1)
                        if last:
                            dve.wait_ge(fsq, m + 1)
                            if m:
                                dve.wait_ge(facc, m)
                            dve.tensor_tensor(tmp[:, 3, :], tmp[:, 3, :], tmp[:, 0, :], ALU.add).then_inc(facc, 1)

            with dve.Fori(0, FF_BLOCKS - 1) as b:
                mlp_block(b, False)
            mlp_block(FF_BLOCKS - 1, True)
            dve.wait_ge(fmean, 1)
            dve.tensor_scalar(xstat[:], PS[0][:, 0:8], EPS, None, ALU.add).then_inc(fmean_out, 1)
            dve.wait_ge(froot, 1)
            dve.reciprocal(xrstd[:], xstat[:]).then_inc(frstd, 1)
            dve.wait_ge(frstd, 1)
            dve.wait_ge(gfin_in, 16)
            dve.wait_ge(w_lo, CH_OUT + KC + 8 * FF_BLOCKS)
            for i in range(8):
                dve.wait_ge(ft_done, i + 1)
                dve.scalar_tensor_tensor(out=y_tile[i], in0=PS[1 + i % 3][:], scalar=xrstd[:, i:i + 1],
                                         in1=tmp[:, 2, :], op0=ALU.mult, op1=ALU.mult).then_inc(y_ok, 1)


def kernel(**inputs):
    import numpy as np
    import concourse.bacc as bacc
    from concourse.bass_utils import run_bass_kernel_spmd

    f = {k: np.asarray(v) for k, v in inputs.items()}
    half = HD // 8
    inv = np.power(np.float32(500000.0), -np.arange(half, dtype=np.float32) * np.float32(2.0) / np.float32(2 * half))
    ang = np.arange(S, dtype=np.float32)[None, :] * inv.astype(np.float32)[:, None]
    rope = np.zeros((P, 2, S), np.float32)
    rope[:, 0] = 1.0
    for h in range(2):
        for part in range(2):
            rows = slice(h * HD + part * half, h * HD + (part + 1) * half)
            rope[rows, 0] = np.cos(ang)
            rope[rows, 1] = np.sin(ang) * (1.0 if part else -1.0)
    arrays = {
        "x": np.ascontiguousarray(f["x"][0]),
        "g_attn": np.ascontiguousarray(f["norm_attn_g"][0].reshape(KC, P).T),
        "w_in": np.ascontiguousarray(f["w_in"][0]),
        "b_forget": np.ascontiguousarray(f["b_forget"][0].reshape(FOX_HEADS, 1)),
        "w_branch": np.concatenate([f["w_branch_a"][0], f["w_branch_b"][0]], axis=0),
        "w_out": np.ascontiguousarray(f["w_out"][0]),
        "g_mlp": np.ascontiguousarray(f["norm_mlp_g"][0].reshape(KC, P).T),
        "w_up": np.ascontiguousarray(f["w_up"][0]),
        "w_down": np.ascontiguousarray(f["w_down"][0]),
        "g_final": np.ascontiguousarray(np.broadcast_to(f["norm_final_g"], (P, D))),
        "rope": rope,
    }
    nc = bacc.Bacc("TRN2", target_bir_lowering=False, num_devices=1)
    args = [nc.dram_tensor(f"in_{k}", a.shape, mybir.dt.from_np(a.dtype), kind="ExternalInput").ap()
            for k, a in arrays.items()]
    out = nc.dram_tensor("out_y", (S, D), F32, kind="ExternalOutput").ap()
    build(nc, *args, out)
    r = run_bass_kernel_spmd(nc, [{f"in_{k}": a for k, a in arrays.items()}], core_ids=[0])
    return r.results[0]["out_y"].reshape(1, S, D)
```
